# Optimizing a Trainium2 kernel written in Bass

```python
import jax
import jax.numpy as jnp
from jax import lax
import numpy as np
import jax, jax.numpy as jnp

D_MODEL = 1024
BATCH = 1
SEQ = 512
DEPTH = 1

GRID_W = 64
CTX_LEN = 256
MIX_WIDTH = D_MODEL
HG_WIDTH = MIX_WIDTH // 2
HG_HEADS = 4
HG_KDIM = 128
HG_KEYS = HG_HEADS * HG_KDIM
HG_VDIM = HG_WIDTH // HG_HEADS
SC_WIDTH = MIX_WIDTH - HG_WIDTH
CONV_W = 3
CHUNK = 32
N_EXPERTS = 16
EC_CAPACITY = 2
EXPERT_DFF = 2 * D_MODEL
N_MOD = 6
EPS = 1e-6
IN_COLS = 3 * HG_KEYS + 2 * HG_WIDTH + 3 * SC_WIDTH


def rms_norm(x, gain):
    xf = x.astype(jnp.float32)
    y = xf * lax.rsqrt(jnp.mean(xf * xf, axis=-1, keepdims=True) + EPS)
    return (y * gain.astype(jnp.float32)).astype(x.dtype)

def modulate(h, shift, scale):
    return h * (1 + scale) + shift

def adaln(cond, w, b):
    return jnp.split(jax.nn.silu(cond) @ w + b, N_MOD, axis=-1)

def dwconv3(u, w):
    pad = [(0, 0)] * (u.ndim - 2) + [(1, 1), (0, 0)]
    up = jnp.pad(u, pad)
    return w[0] * up[..., :-2, :] + w[1] * up[..., 1:-1, :] + w[2] * up[..., 2:, :]

def split_proj(z):
    cuts = [HG_KEYS, 2 * HG_KEYS, 3 * HG_KEYS, 3 * HG_KEYS + HG_WIDTH, 3 * HG_KEYS + 2 * HG_WIDTH,
            3 * HG_KEYS + 2 * HG_WIDTH + SC_WIDTH, 3 * HG_KEYS + 2 * HG_WIDTH + 2 * SC_WIDTH]
    return jnp.split(z, cuts, axis=-1)

def hgrn2_gates(zf, lb):
    b, t, _ = zf.shape
    f = lb + (1.0 - lb) * jax.nn.sigmoid(zf.astype(jnp.float32))
    return jnp.log(f).reshape(b, t, HG_HEADS, HG_KDIM), (1.0 - f).reshape(b, t, HG_HEADS, HG_KDIM)

def gla_chunked(q, k, v, log_f, s0):
    b, t, h, _ = q.shape
    dv = v.shape[-1]
    n = t // CHUNK
    q, k, v, log_f = [a.astype(jnp.float32).reshape(b, n, CHUNK, h, a.shape[-1]) for a in (q, k, v, log_f)]
    cum = jnp.cumsum(log_f, axis=2)
    last = cum[:, :, -1:]
    q_dec = q * jnp.exp(cum)
    k_inv = k * jnp.exp(-cum)
    k_end = k * jnp.exp(last - cum)
    lower = jnp.tril(jnp.ones((CHUNK, CHUNK), jnp.bool_))
    scores = jnp.where(lower, jnp.einsum('bnihd,bnjhd->bnhij', q_dec, k_inv), 0.0)
    o_intra = jnp.einsum('bnhij,bnjhv->bnihv', scores, v)
    kv = jnp.einsum('bnjhd,bnjhv->bnhdv', k_end, v)
    decay = jnp.exp(last[:, :, 0])

    def step(s, inp):
        dec, kv_n = inp
        return dec[..., None] * s + kv_n, s

    s_final, s_prev = lax.scan(step, s0.astype(jnp.float32),
                               (jnp.moveaxis(decay, 1, 0), jnp.moveaxis(kv, 1, 0)))
    o_inter = jnp.einsum('bnihd,nbhdv->bnihv', q_dec, s_prev)
    return (o_intra + o_inter).reshape(b, t, h, dv), s_final

def gla_final_state(k, v, log_f):
    cum = jnp.cumsum(log_f, axis=1)
    return jnp.einsum('bthd,bthv->bhdv', k * jnp.exp(cum[:, -1:] - cum), v)

def hgrn2_mix(q, i, zf_f, zf_b, g, lb_f, lb_b, s0_f, s0_b, gain):
    b, t, _ = q.shape
    qh = q.reshape(b, t, HG_HEADS, HG_KDIM)
    vh = i.reshape(b, t, HG_HEADS, HG_VDIM)
    logf_f, k_f = hgrn2_gates(zf_f, lb_f)
    logf_b, k_b = hgrn2_gates(zf_b, lb_b)
    rev = lambda a: jnp.flip(a, axis=1)
    o_f, s_f = gla_chunked(qh, k_f, vh, logf_f, s0_f)
    o_b, s_b = gla_chunked(rev(qh), rev(k_b), rev(vh), rev(logf_b), s0_b)
    o = (o_f + rev(o_b)).astype(q.dtype)
    o = rms_norm(o, gain) * jax.nn.silu(g.reshape(b, t, HG_HEADS, HG_VDIM))
    return o.reshape(b, t, HG_WIDTH), s_f, s_b

def hgrn2_context_states(zf_f, zf_b, i, lb_f, lb_b):
    b, t, _ = i.shape
    vh = i.astype(jnp.float32).reshape(b, t, HG_HEADS, HG_VDIM)
    logf_f, k_f = hgrn2_gates(zf_f, lb_f)
    logf_b, k_b = hgrn2_gates(zf_b, lb_b)
    s_f = gla_final_state(k_f, vh, logf_f)
    s_b = gla_final_state(jnp.flip(k_b, 1), jnp.flip(vh, 1), jnp.flip(logf_b, 1))
    return s_f, s_b

def token_mix(h, w_in_l, w_out_l, lb_f, lb_b, hg_gain, conv_l, s0_f, s0_b, grid_rows):
    b, t, _ = h.shape
    q, zf_f, zf_b, i, g, gate_b, gate_c, v = split_proj(h @ w_in_l)
    o_hg, s_f, s_b = hgrn2_mix(q, i, zf_f, zf_b, g, lb_f, lb_b, s0_f, s0_b, hg_gain)
    u = gate_c * v
    if grid_rows is None:
        y = dwconv3(u, conv_l)
    else:
        y = dwconv3(u.reshape(b, grid_rows, GRID_W, SC_WIDTH), conv_l).reshape(b, t, SC_WIDTH)
    y = gate_b * y
    return jnp.concatenate([o_hg, y], axis=-1) @ w_out_l, s_f, s_b

def expert_choice_ffn(h, w_router, w_gate, w_up, w_down):
    b, t, d = h.shape
    cap = EC_CAPACITY * t // N_EXPERTS
    aff = jax.nn.softmax(jnp.einsum('btd,de->bte', h, w_router).astype(jnp.float32), axis=-1)
    gate, idx = lax.top_k(jnp.swapaxes(aff, 1, 2), cap)
    xs = jax.vmap(lambda hb, ib: hb[ib])(h, idx)
    hid = jax.nn.silu(jnp.einsum('becd,edf->becf', xs, w_gate)) * jnp.einsum('becd,edf->becf', xs, w_up)
    ys = jnp.einsum('becf,efd->becd', hid, w_down) * gate[..., None].astype(h.dtype)
    return jax.vmap(lambda ib, yb: jnp.zeros((t, d), yb.dtype).at[ib.reshape(-1)].add(yb.reshape(-1, d)))(idx, ys)

def first_inputs(seed: int = 0) -> dict:
    key = jax.random.key(seed)
    ks = jax.random.split(key, 20)
    nrm = lambda k, shape, s: jax.random.normal(k, shape, jnp.float32) * s
    return {
        'x': nrm(ks[0], (BATCH, SEQ, D_MODEL), 1.0),
        'c': nrm(ks[1], (BATCH, D_MODEL), 1.0),
        'ctx': nrm(ks[2], (BATCH, CTX_LEN, D_MODEL), 1.0),
        'c_ctx': nrm(ks[3], (D_MODEL,), 1.0),
        'w_ada': nrm(ks[4], (DEPTH, D_MODEL, N_MOD * D_MODEL), 0.5 * D_MODEL ** -0.5),
        'b_ada': nrm(ks[5], (DEPTH, N_MOD * D_MODEL), 0.02),
        'norm_mix': 1.0 + nrm(ks[6], (DEPTH, D_MODEL), 0.02),
        'norm_ffn': 1.0 + nrm(ks[7], (DEPTH, D_MODEL), 0.02),
        'w_in': nrm(ks[8], (DEPTH, D_MODEL, IN_COLS), D_MODEL ** -0.5),
        'lb_logits': nrm(ks[9], (DEPTH + 1, 2, HG_KEYS), 0.3),
        'hg_norm': 1.0 + nrm(ks[10], (DEPTH, HG_VDIM), 0.02),
        'conv_w': nrm(ks[11], (DEPTH, CONV_W, SC_WIDTH), CONV_W ** -0.5),
        'w_out': nrm(ks[12], (DEPTH, MIX_WIDTH, D_MODEL), MIX_WIDTH ** -0.5),
        'w_router': nrm(ks[13], (DEPTH, D_MODEL, N_EXPERTS), D_MODEL ** -0.5),
        'w_gate': nrm(ks[14], (DEPTH, N_EXPERTS, D_MODEL, EXPERT_DFF), D_MODEL ** -0.5),
        'w_up': nrm(ks[15], (DEPTH, N_EXPERTS, D_MODEL, EXPERT_DFF), D_MODEL ** -0.5),
        'w_down': nrm(ks[16], (DEPTH, N_EXPERTS, EXPERT_DFF, D_MODEL), EXPERT_DFF ** -0.5),
        'norm_final': 1.0 + nrm(ks[17], (D_MODEL,), 0.02),
    }

def first_block(x, c, ctx, c_ctx, w_ada, b_ada, norm_mix, norm_ffn, w_in, lb_logits, hg_norm, conv_w,
              w_out, w_router, w_gate, w_up, w_down, norm_final):
    b = x.shape[0]
    rows = x.shape[1] // GRID_W
    lower_bounds = jnp.cumsum(jax.nn.softmax(lb_logits.astype(jnp.float32), axis=0), axis=0)
    cx = ctx
    for l in range(DEPTH):
        sh1, sc1, g1, sh2, sc2, g2 = [m[:, None] for m in adaln(c, w_ada[l], b_ada[l])]
        csh1, csc1, cg1, csh2, csc2, cg2 = adaln(c_ctx, w_ada[l], b_ada[l])
        lb_f, lb_b = lower_bounds[l, 0], lower_bounds[l, 1]
        hc = modulate(rms_norm(cx, norm_mix[l]), csh1, csc1)
        if l == DEPTH - 1:
            zf_f, zf_b, i_c = jnp.split(hc @ w_in[l][:, HG_KEYS:3 * HG_KEYS + HG_WIDTH],
                                        [HG_KEYS, 2 * HG_KEYS], axis=-1)
            s_f, s_b = hgrn2_context_states(zf_f, zf_b, i_c, lb_f, lb_b)
        else:
            zero = jnp.zeros((b, HG_HEADS, HG_KDIM, HG_VDIM), jnp.float32)
            mc, s_f, s_b = token_mix(hc, w_in[l], w_out[l], lb_f, lb_b, hg_norm[l], conv_w[l],
                                     zero, zero, None)
            cx = cx + cg1 * mc
            hc2 = modulate(rms_norm(cx, norm_ffn[l]), csh2, csc2)
            cx = cx + cg2 * expert_choice_ffn(hc2, w_router[l], w_gate[l], w_up[l], w_down[l])
        hx = modulate(rms_norm(x, norm_mix[l]), sh1, sc1)
        mx, _, _ = token_mix(hx, w_in[l], w_out[l], lb_f, lb_b, hg_norm[l], conv_w[l], s_f, s_b, rows)
        x = x + g1 * mx
        hx2 = modulate(rms_norm(x, norm_ffn[l]), sh2, sc2)
        x = x + g2 * expert_choice_ffn(hx2, w_router[l], w_gate[l], w_up[l], w_down[l])
    return rms_norm(x, norm_final)


D_MIX = D_MODEL
HEAD_DIM = 64
RWKV_HEADS = 6
D_RWKV = RWKV_HEADS * HEAD_DIM
DECAY_LORA = 64
AAA_LORA = 64
GATE_LORA = 128
RWKV_LNX_EPS = 64e-5
MOBA_HEADS = 6
D_MOBA = MOBA_HEADS * HEAD_DIM
MOBA_BLOCK = 256
MOBA_TOPK = 3
MOBA_QCHUNK = 32
GMLP_GROUPS = 4
D_GMLP = GMLP_GROUPS * HEAD_DIM
GMLP_CHUNK = 128
D_FF = ((8 * D_MODEL // 3 + 255) // 256) * 256
NORM_EPS = 1e-6

A_COLS = 3 * D_RWKV + DECAY_LORA + AAA_LORA + GATE_LORA
B_COLS = 3 * D_MOBA
C_COLS = 2 * D_GMLP
D_IN = A_COLS + B_COLS + C_COLS


def rmsnorm(x, g):
    xf = x.astype(jnp.float32)
    y = xf * lax.rsqrt(jnp.mean(xf * xf, axis=-1, keepdims=True) + NORM_EPS)
    return (y * g.astype(jnp.float32)).astype(x.dtype)

def rwkv7_mixer(ya, mu, w0, w2, a0, a2, g2, k_k, k_a, r_k, lnx_g, lnx_b):
    B, S, _ = ya.shape
    H, D = RWKV_HEADS, HEAD_DIM
    prev = jnp.pad(ya, ((0, 0), (1, 0), (0, 0)))[:, :-1]
    ya = ya + mu * (prev - ya)
    r, k, v, wd, ad, gd = jnp.split(
        ya, [D_RWKV, 2 * D_RWKV, 3 * D_RWKV, 3 * D_RWKV + DECAY_LORA,
             3 * D_RWKV + DECAY_LORA + AAA_LORA], axis=-1)
    w = -jax.nn.softplus(-(w0 + jnp.tanh(wd) @ w2).astype(jnp.float32)) - 0.5
    decay = jnp.exp(-jnp.exp(w))
    a = jax.nn.sigmoid((a0 + ad @ a2).astype(jnp.float32))
    g = jax.nn.sigmoid(gd) @ g2
    heads = lambda t: t.astype(jnp.float32).reshape(B, S, H, D)
    kk = heads(k * k_k)
    kk = kk / jnp.maximum(jnp.linalg.norm(kk, axis=-1, keepdims=True), 1e-12)
    k = k * (1.0 + (a - 1.0) * k_a)
    rh, kh, vh, ah, dh = heads(r), heads(k), heads(v), heads(a), heads(decay)

    def step(state, inp):
        r_t, w_t, k_t, v_t, kk_t, a_t = inp
        sa = jnp.einsum('bhij,bhj->bhi', state, -kk_t)
        state = (state * w_t[:, :, None, :]
                 + sa[..., :, None] * (kk_t * a_t)[:, :, None, :]
                 + v_t[..., :, None] * k_t[:, :, None, :])
        return state, jnp.einsum('bhij,bhj->bhi', state, r_t)

    xs = tuple(jnp.moveaxis(t, 1, 0) for t in (rh, dh, kh, vh, kk, ah))
    s0 = jnp.zeros((B, H, D, D), jnp.float32)
    _, y = lax.scan(step, s0, xs)
    y = jnp.moveaxis(y, 0, 1)
    mean = jnp.mean(y, axis=-1, keepdims=True)
    var = jnp.mean(jnp.square(y - mean), axis=-1, keepdims=True)
    y = ((y - mean) * lax.rsqrt(var + RWKV_LNX_EPS)).reshape(B, S, D_RWKV)
    y = y * lnx_g + lnx_b
    bonus = jnp.sum(rh * kh * r_k.astype(jnp.float32), axis=-1, keepdims=True) * vh
    out = (y + bonus.reshape(B, S, D_RWKV)) * g.astype(jnp.float32)
    return out.astype(ya.dtype)

def moba_mixer(q, k, v):
    B, S, _ = q.shape
    H, D = MOBA_HEADS, HEAD_DIM
    q, k, v = (t.reshape(B, S, H, D).transpose(0, 2, 1, 3) for t in (q, k, v))
    nb = -(-S // MOBA_BLOCK)
    pad = nb * MOBA_BLOCK - S
    kb = jnp.pad(k, ((0, 0), (0, 0), (0, pad), (0, 0))).reshape(B, H, nb, MOBA_BLOCK, D)
    vb = jnp.pad(v, ((0, 0), (0, 0), (0, pad), (0, 0))).reshape(B, H, nb, MOBA_BLOCK, D)
    pos = jnp.arange(S)
    qblk = pos // MOBA_BLOCK
    own = jnp.broadcast_to(qblk[None, None, :, None], (B, H, S, 1))
    n_top = min(MOBA_TOPK, nb - 1)
    if n_top > 0:
        kbar = jnp.mean(kb.astype(jnp.float32), axis=3)
        blk_scores = jnp.einsum('bhsd,bhnd->bhsn', q.astype(jnp.float32), kbar)
        past = jnp.arange(nb)[None, :] < qblk[:, None]
        blk_scores = jnp.where(past, blk_scores, -jnp.inf)
        _, top = lax.top_k(blk_scores, n_top)
        sel = jnp.concatenate([top, own], axis=-1)
        sel_valid = jnp.concatenate(
            [top < qblk[None, None, :, None], jnp.ones_like(own, dtype=bool)], axis=-1)
    else:
        sel = own
        sel_valid = jnp.ones_like(own, dtype=bool)
    nsel = sel.shape[-1]
    nq = S // MOBA_QCHUNK
    q_c = jnp.moveaxis(q.reshape(B, H, nq, MOBA_QCHUNK, D), 2, 0)
    sel_c = jnp.moveaxis(sel.reshape(B, H, nq, MOBA_QCHUNK, nsel), 2, 0)
    val_c = jnp.moveaxis(sel_valid.reshape(B, H, nq, MOBA_QCHUNK, nsel), 2, 0)
    pos_c = pos.reshape(nq, MOBA_QCHUNK)
    bi = jnp.arange(B)[:, None, None, None]
    hi = jnp.arange(H)[None, :, None, None]
    scale = HEAD_DIM ** -0.5

    def attend(args):
        qq, ss, vv, pp = args
        kg = kb[bi, hi, ss]
        vg = vb[bi, hi, ss]
        logits = jnp.einsum('bhqd,bhqnkd->bhqnk', qq, kg).astype(jnp.float32) * scale
        kpos = ss[..., None] * MOBA_BLOCK + jnp.arange(MOBA_BLOCK)
        mask = vv[..., None] & (kpos <= pp[None, None, :, None, None])
        logits = jnp.where(mask, logits, -jnp.inf)
        p = jax.nn.softmax(logits.reshape(B, H, MOBA_QCHUNK, nsel * MOBA_BLOCK), axis=-1)
        p = p.reshape(B, H, MOBA_QCHUNK, nsel, MOBA_BLOCK).astype(vg.dtype)
        return jnp.einsum('bhqnk,bhqnkd->bhqd', p, vg)

    o = lax.map(attend, (q_c, sel_c, val_c, pos_c))
    o = jnp.moveaxis(o, 0, 2).reshape(B, H, S, D).transpose(0, 2, 1, 3)
    return o.reshape(B, S, D_MOBA)

def gmlp_mixer(u, v, ln_g, ln_b, w_s, b_s):
    B, S, _ = u.shape
    u = jax.nn.gelu(u)
    v = jax.nn.gelu(v)
    vf = v.astype(jnp.float32)
    mean = jnp.mean(vf, axis=-1, keepdims=True)
    var = jnp.mean(jnp.square(vf - mean), axis=-1, keepdims=True)
    v = (((vf - mean) * lax.rsqrt(var + NORM_EPS)) * ln_g + ln_b).astype(u.dtype)
    nc = S // GMLP_CHUNK
    vc = v.reshape(B, nc, GMLP_CHUNK, GMLP_GROUPS, HEAD_DIM)
    tril = jnp.tril(jnp.ones((GMLP_CHUNK, GMLP_CHUNK), dtype=bool))
    w_causal = jnp.where(tril[None], w_s, 0.0)
    s = jnp.einsum('gts,bcsgd->bctgd', w_causal, vc) + b_s.T[:, :, None]
    return u * s.reshape(B, S, D_GMLP)

def second_inputs(seed: int = 0) -> dict:
    key = jax.random.key(seed)
    ks = jax.random.split(key, 24)
    n = lambda k, shape, s: jax.random.normal(k, shape, jnp.float32) * s
    L = DEPTH
    return {
        "x": n(ks[0], (BATCH, SEQ, D_MODEL), 1.0),
        "pre_mix_g": 1.0 + n(ks[1], (L, D_MODEL), 0.02),
        "w_in": n(ks[2], (L, D_MODEL, D_IN), D_MODEL ** -0.5),
        "rwkv_mu": jax.random.uniform(ks[3], (L, A_COLS), jnp.float32),
        "rwkv_w0": jax.random.uniform(ks[4], (L, D_RWKV), jnp.float32, -5.0, 1.0),
        "rwkv_w2": n(ks[5], (L, DECAY_LORA, D_RWKV), 0.1),
        "rwkv_a0": n(ks[6], (L, D_RWKV), 0.1),
        "rwkv_a2": n(ks[7], (L, AAA_LORA, D_RWKV), 0.5 * AAA_LORA ** -0.5),
        "rwkv_g2": n(ks[8], (L, GATE_LORA, D_RWKV), GATE_LORA ** -0.5),
        "rwkv_k_k": 0.85 + n(ks[9], (L, D_RWKV), 0.02),
        "rwkv_k_a": 1.0 + n(ks[10], (L, D_RWKV), 0.02),
        "rwkv_r_k": n(ks[11], (L, RWKV_HEADS, HEAD_DIM), 0.1),
        "rwkv_lnx_g": 1.0 + n(ks[12], (L, D_RWKV), 0.02),
        "rwkv_lnx_b": n(ks[13], (L, D_RWKV), 0.02),
        "gmlp_ln_g": 1.0 + n(ks[14], (L, D_GMLP), 0.02),
        "gmlp_ln_b": n(ks[15], (L, D_GMLP), 0.02),
        "gmlp_w_s": n(ks[16], (L, GMLP_GROUPS, GMLP_CHUNK, GMLP_CHUNK), GMLP_CHUNK ** -0.5),
        "gmlp_b_s": 1.0 + n(ks[17], (L, GMLP_GROUPS, GMLP_CHUNK), 0.01),
        "w_out": n(ks[18], (L, D_MIX, D_MODEL), D_MIX ** -0.5),
        "post_mix_g": 1.0 + n(ks[19], (L, D_MODEL), 0.02),
        "pre_ffn_g": 1.0 + n(ks[20], (L, D_MODEL), 0.02),
        "w_ffn_in": n(ks[21], (L, D_MODEL, 2 * D_FF), D_MODEL ** -0.5),
        "w_ffn_out": n(ks[22], (L, D_FF, D_MODEL), D_FF ** -0.5),
        "post_ffn_g": 1.0 + n(ks[23], (L, D_MODEL), 0.02),
    }

def second_block(x, pre_mix_g, w_in, rwkv_mu, rwkv_w0, rwkv_w2, rwkv_a0, rwkv_a2, rwkv_g2,
              rwkv_k_k, rwkv_k_a, rwkv_r_k, rwkv_lnx_g, rwkv_lnx_b, gmlp_ln_g, gmlp_ln_b,
              gmlp_w_s, gmlp_b_s, w_out, post_mix_g, pre_ffn_g, w_ffn_in, w_ffn_out,
              post_ffn_g):
    for l in range(DEPTH):
        h = rmsnorm(x, pre_mix_g[l])
        proj = h @ w_in[l]
        ya, yb, yc = jnp.split(proj, [A_COLS, A_COLS + B_COLS], axis=-1)
        a_out = rwkv7_mixer(ya, rwkv_mu[l], rwkv_w0[l], rwkv_w2[l], rwkv_a0[l],
                            rwkv_a2[l], rwkv_g2[l], rwkv_k_k[l], rwkv_k_a[l],
                            rwkv_r_k[l], rwkv_lnx_g[l], rwkv_lnx_b[l])
        qb, kb, vb = jnp.split(yb, 3, axis=-1)
        b_out = moba_mixer(qb, kb, vb)
        u, v = jnp.split(yc, 2, axis=-1)
        c_out = gmlp_mixer(u, v, gmlp_ln_g[l], gmlp_ln_b[l], gmlp_w_s[l], gmlp_b_s[l])
        mix = jnp.concatenate([a_out, b_out, c_out], axis=-1) @ w_out[l]
        x = x + rmsnorm(mix, post_mix_g[l])
        h = rmsnorm(x, pre_ffn_g[l])
        gate, up = jnp.split(h @ w_ffn_in[l], 2, axis=-1)
        f = (jax.nn.silu(gate) * up) @ w_ffn_out[l]
        x = x + rmsnorm(f, post_ffn_g[l])
    return x


_first_inputs = second_inputs


def second_inputs(seed=0):
    import zlib

    import numpy as np

    out = dict(_first_inputs(seed))
    spreads = {}
    factors = {'rwkv_k_k': 7.83,
     'rwkv_k_a': 5.169,
     'rwkv_lnx_g': 5.408,
     'rwkv_lnx_b': 5.744,
     'gmlp_ln_g': 8.0,
     'gmlp_ln_b': 8.0,
     'gmlp_b_s': 8.0,
     'post_mix_g': 3.443,
     'pre_ffn_g': 3.555,
     'post_ffn_g': 5.051}
    for name, (base, spread) in spreads.items():
        noise = np.random.default_rng([zlib.crc32(name.encode()), seed]).standard_normal(out[name].shape)
        drawn = base * np.exp(spread * noise) if base else spread * noise
        out[name] = __import__('jax').numpy.asarray(drawn.astype(out[name].dtype))
    for name, factor in factors.items():
        out[name] = (out[name] * factor).astype(out[name].dtype)
    return out


_narrow_inputs = second_inputs


def second_inputs(seed=0):

    out = dict(_narrow_inputs(seed))
    wider = {'rwkv_k_k': 7.56,
     'rwkv_k_a': 3.11,
     'rwkv_lnx_g': 4.99,
     'rwkv_lnx_b': 5.03,
     'gmlp_ln_g': 5.5,
     'gmlp_ln_b': 5.88,
     'gmlp_b_s': 8.06,
     'post_ffn_g': 4.01}
    for name, times in wider.items():
        mean = out[name].mean()
        out[name] = (mean + times * (out[name] - mean)).astype(out[name].dtype)
    return out


N_HEADS = 8
QK_NOPE_DIM = 128
QK_ROPE_DIM = 64
V_HEAD_DIM = 128
Q_LORA_RANK = 3 * D_MODEL // 8
KV_LORA_RANK = D_MODEL // 4
ROPE_THETA = 10000.0
Q_BLOCK = 128
CONV_CHANNELS = D_MODEL
CONV_WIDTH = 31
D_FF_3 = 4 * D_MODEL
N_BRANCHES = 2
IN_SIZES = (Q_LORA_RANK, KV_LORA_RANK, QK_ROPE_DIM, 2 * CONV_CHANNELS, N_BRANCHES * D_MODEL)
IN_OFFSETS = tuple(int(o) for o in np.cumsum(IN_SIZES)[:-1])
D_IN_3 = int(sum(IN_SIZES))


def rms_norm_3(x, g):
    x32 = x.astype(jnp.float32)
    y = x32 * lax.rsqrt(jnp.mean(x32 * x32, axis=-1, keepdims=True) + EPS)
    return y.astype(x.dtype) * g

def layer_norm(x, g, b):
    x32 = x.astype(jnp.float32)
    mu = jnp.mean(x32, axis=-1, keepdims=True)
    xc = x32 - mu
    var = jnp.mean(xc * xc, axis=-1, keepdims=True)
    y = xc * lax.rsqrt(var + EPS)
    return y.astype(x.dtype) * g + b

def rope_tables(positions):
    inv_freq = ROPE_THETA ** (-jnp.arange(0, QK_ROPE_DIM, 2, dtype=jnp.float32) / QK_ROPE_DIM)
    ang = positions.astype(jnp.float32)[..., None] * inv_freq
    return jnp.cos(ang), jnp.sin(ang)

def apply_rope(x, cos, sin):
    half = x.shape[-1] // 2
    x1, x2 = x[..., :half], x[..., half:]
    cos = cos.astype(x.dtype)
    sin = sin.astype(x.dtype)
    return jnp.concatenate([x1 * cos - x2 * sin, x2 * cos + x1 * sin], axis=-1)

def causal_block_attention(q_nope, q_rope, k_nope, k_rope, v):
    B, H, S, Dn = q_nope.shape
    Dr = q_rope.shape[-1]
    Dv = v.shape[-1]
    n_blk = S // Q_BLOCK
    qn = q_nope.reshape(B, H, n_blk, Q_BLOCK, Dn).transpose(2, 0, 1, 3, 4)
    qr = q_rope.reshape(B, H, n_blk, Q_BLOCK, Dr).transpose(2, 0, 1, 3, 4)
    scale = (Dn + Dr) ** -0.5
    key_idx = jnp.arange(S)

    def one_block(args):
        qn_b, qr_b, blk = args
        s = jnp.einsum('bhqd,bhkd->bhqk', qn_b, k_nope) + jnp.einsum('bhqd,bkd->bhqk', qr_b, k_rope)
        s = s.astype(jnp.float32) * scale
        q_idx = blk * Q_BLOCK + jnp.arange(Q_BLOCK)
        mask = key_idx[None, :] <= q_idx[:, None]
        s = jnp.where(mask, s, -jnp.inf)
        p = jax.nn.softmax(s, axis=-1).astype(v.dtype)
        return jnp.einsum('bhqk,bhkd->bhqd', p, v)

    out = lax.map(one_block, (qn, qr, jnp.arange(n_blk)))
    return out.transpose(1, 0, 3, 2, 4).reshape(B, S, H * Dv)

def hybrid_mixer(h, cos, sin, w_in, q_norm, w_uq, kv_norm, w_uk, w_uv, w_o_attn,
                 conv_w, conv_b, conv_ln_g, conv_ln_b, w_pw2, b_pw2, w_out):
    B, S, _ = h.shape
    z = h @ w_in
    c_q, c_kv, k_r, u_glu, gate_logits = jnp.split(z, IN_OFFSETS, axis=-1)

    q = (rms_norm_3(c_q, q_norm) @ w_uq).reshape(B, S, N_HEADS, QK_NOPE_DIM + QK_ROPE_DIM)
    q_nope = q[..., :QK_NOPE_DIM]
    q_rope = apply_rope(q[..., QK_NOPE_DIM:], cos[:, :, None, :], sin[:, :, None, :])
    c_kv_n = rms_norm_3(c_kv, kv_norm)
    k_nope = jnp.einsum('bsc,chd->bhsd', c_kv_n, w_uk)
    v = jnp.einsum('bsc,chd->bhsd', c_kv_n, w_uv)
    k_rope = apply_rope(k_r, cos, sin)
    attn = causal_block_attention(q_nope.transpose(0, 2, 1, 3), q_rope.transpose(0, 2, 1, 3),
                                  k_nope, k_rope, v)
    y_attn = attn @ w_o_attn

    a, b = jnp.split(u_glu, 2, axis=-1)
    u = a * jax.nn.sigmoid(b)
    u = lax.conv_general_dilated(u, conv_w, window_strides=(1,),
                                 padding=[(CONV_WIDTH - 1, 0)],
                                 dimension_numbers=('NWC', 'WIO', 'NWC'),
                                 feature_group_count=CONV_CHANNELS) + conv_b
    u = jax.nn.silu(layer_norm(u, conv_ln_g, conv_ln_b))
    y_conv = u @ w_pw2 + b_pw2

    g_attn, g_conv = jnp.split(gate_logits, N_BRANCHES, axis=-1)
    merged = jax.nn.sigmoid(g_attn) * y_attn + jax.nn.sigmoid(g_conv) * y_conv
    return merged @ w_out

def squared_relu_mlp(h, w_ff1, w_ff2):
    return jnp.square(jax.nn.relu(h @ w_ff1)) @ w_ff2

def third_inputs(seed: int = 0) -> dict:
    key = jax.random.key(seed)
    ks = jax.random.split(key, 24)
    f32 = jnp.float32

    def nrm(k, shape, scale):
        return jax.random.normal(k, shape, f32) * scale

    def gain(k, shape):
        return 1.0 + 0.01 * jax.random.normal(k, shape, f32)

    L = DEPTH
    x = jax.random.normal(ks[0], (BATCH, SEQ, D_MODEL), f32)
    offset = jax.random.randint(ks[1], (BATCH, 1), 0, 1024, dtype=jnp.int32)
    positions = (offset + jnp.arange(SEQ, dtype=jnp.int32)[None, :]).astype(jnp.int32)
    return {
        "x": x,
        "positions": positions,
        "norm_mix_pre": gain(ks[2], (L, D_MODEL)),
        "w_in": nrm(ks[3], (L, D_MODEL, D_IN_3), D_MODEL ** -0.5),
        "q_norm": gain(ks[4], (L, Q_LORA_RANK)),
        "w_uq": nrm(ks[5], (L, Q_LORA_RANK, N_HEADS * (QK_NOPE_DIM + QK_ROPE_DIM)), Q_LORA_RANK ** -0.5),
        "kv_norm": gain(ks[6], (L, KV_LORA_RANK)),
        "w_uk": nrm(ks[7], (L, KV_LORA_RANK, N_HEADS, QK_NOPE_DIM), KV_LORA_RANK ** -0.5),
        "w_uv": nrm(ks[8], (L, KV_LORA_RANK, N_HEADS, V_HEAD_DIM), KV_LORA_RANK ** -0.5),
        "w_o_attn": nrm(ks[9], (L, N_HEADS * V_HEAD_DIM, D_MODEL), (N_HEADS * V_HEAD_DIM) ** -0.5),
        "conv_w": nrm(ks[10], (L, CONV_WIDTH, 1, CONV_CHANNELS), CONV_WIDTH ** -0.5),
        "conv_b": nrm(ks[11], (L, CONV_CHANNELS), 0.01),
        "conv_ln_g": gain(ks[12], (L, CONV_CHANNELS)),
        "conv_ln_b": nrm(ks[13], (L, CONV_CHANNELS), 0.01),
        "w_pw2": nrm(ks[14], (L, CONV_CHANNELS, D_MODEL), CONV_CHANNELS ** -0.5),
        "b_pw2": nrm(ks[15], (L, D_MODEL), 0.01),
        "w_out": nrm(ks[16], (L, D_MODEL, D_MODEL), D_MODEL ** -0.5),
        "norm_mix_post": gain(ks[17], (L, D_MODEL)),
        "norm_mlp_pre": gain(ks[18], (L, D_MODEL)),
        "w_ff1": nrm(ks[19], (L, D_MODEL, D_FF_3), D_MODEL ** -0.5),
        "w_ff2": nrm(ks[20], (L, D_FF_3, D_MODEL), D_FF_3 ** -0.5),
        "norm_mlp_post": gain(ks[21], (L, D_MODEL)),
    }

def third_block(x, positions, norm_mix_pre, w_in, q_norm, w_uq, kv_norm, w_uk, w_uv, w_o_attn,
              conv_w, conv_b, conv_ln_g, conv_ln_b, w_pw2, b_pw2, w_out, norm_mix_post,
              norm_mlp_pre, w_ff1, w_ff2, norm_mlp_post):
    cos, sin = rope_tables(positions)
    for l in range(DEPTH):
        h = rms_norm_3(x, norm_mix_pre[l])
        m = hybrid_mixer(h, cos, sin, w_in[l], q_norm[l], w_uq[l], kv_norm[l], w_uk[l], w_uv[l],
                         w_o_attn[l], conv_w[l], conv_b[l], conv_ln_g[l], conv_ln_b[l],
                         w_pw2[l], b_pw2[l], w_out[l])
        x = x + rms_norm_3(m, norm_mix_post[l])
        f = squared_relu_mlp(rms_norm_3(x, norm_mlp_pre[l]), w_ff1[l], w_ff2[l])
        x = x + rms_norm_3(f, norm_mlp_post[l])
    return x


_first_inputs_3 = third_inputs


def third_inputs(seed=0):
    import zlib

    import numpy as np

    out = dict(_first_inputs_3(seed))
    spreads = {}
    factors = {'norm_mix_pre': 6.226,
     'q_norm': 29.089,
     'kv_norm': 31.679,
     'conv_b': 32.04,
     'conv_ln_g': 200.0,
     'conv_ln_b': 200.0,
     'b_pw2': 200.0,
     'norm_mix_post': 200.0,
     'norm_mlp_pre': 200.0,
     'norm_mlp_post': 200.0}
    for name, (base, spread) in spreads.items():
        noise = np.random.default_rng([zlib.crc32(name.encode()), seed]).standard_normal(out[name].shape)
        drawn = base * np.exp(spread * noise) if base else spread * noise
        out[name] = __import__('jax').numpy.asarray(drawn.astype(out[name].dtype))
    for name, factor in factors.items():
        out[name] = (out[name] * factor).astype(out[name].dtype)
    return out


_narrow_inputs_3 = third_inputs


def third_inputs(seed=0):

    out = dict(_narrow_inputs_3(seed))
    wider = {'conv_ln_g': 6.25,
     'conv_ln_b': 5.95,
     'b_pw2': 4.38,
     'norm_mix_post': 6.0,
     'norm_mlp_pre': 8.15,
     'norm_mlp_post': 8.89}
    for name, times in wider.items():
        mean = out[name].mean()
        out[name] = (mean + times * (out[name] - mean)).astype(out[name].dtype)
    return out


def setup_inputs(seed=0):
    out = dict(first_inputs(seed))
    for name, value in second_inputs(seed + 1).items():
        if name != "x":
            out[name + "_2"] = value
    for name, value in third_inputs(seed + 2).items():
        if name != "x":
            out[name + "_3"] = value
    return out


def reference(
    x, c, ctx, c_ctx, w_ada, b_ada, norm_mix, norm_ffn, w_in, lb_logits, hg_norm, conv_w, w_out,
    w_router, w_gate, w_up, w_down, norm_final, pre_mix_g_2, w_in_2, rwkv_mu_2, rwkv_w0_2,
    rwkv_w2_2, rwkv_a0_2, rwkv_a2_2, rwkv_g2_2, rwkv_k_k_2, rwkv_k_a_2, rwkv_r_k_2,
    rwkv_lnx_g_2, rwkv_lnx_b_2, gmlp_ln_g_2, gmlp_ln_b_2, gmlp_w_s_2, gmlp_b_s_2, w_out_2,
    post_mix_g_2, pre_ffn_g_2, w_ffn_in_2, w_ffn_out_2, post_ffn_g_2, positions_3,
    norm_mix_pre_3, w_in_3, q_norm_3, w_uq_3, kv_norm_3, w_uk_3, w_uv_3, w_o_attn_3, conv_w_3,
    conv_b_3, conv_ln_g_3, conv_ln_b_3, w_pw2_3, b_pw2_3, w_out_3, norm_mix_post_3,
    norm_mlp_pre_3, w_ff1_3, w_ff2_3, norm_mlp_post_3,
):
    x = first_block(
        x, c, ctx, c_ctx, w_ada, b_ada, norm_mix, norm_ffn, w_in, lb_logits, hg_norm, conv_w,
        w_out, w_router, w_gate, w_up, w_down, norm_final,
    )
    x = second_block(
        x, pre_mix_g_2, w_in_2, rwkv_mu_2, rwkv_w0_2, rwkv_w2_2, rwkv_a0_2, rwkv_a2_2,
        rwkv_g2_2, rwkv_k_k_2, rwkv_k_a_2, rwkv_r_k_2, rwkv_lnx_g_2, rwkv_lnx_b_2, gmlp_ln_g_2,
        gmlp_ln_b_2, gmlp_w_s_2, gmlp_b_s_2, w_out_2, post_mix_g_2, pre_ffn_g_2, w_ffn_in_2,
        w_ffn_out_2, post_ffn_g_2,
    )
    return third_block(
        x, positions_3, norm_mix_pre_3, w_in_3, q_norm_3, w_uq_3, kv_norm_3, w_uk_3, w_uv_3,
        w_o_attn_3, conv_w_3, conv_b_3, conv_ln_g_3, conv_ln_b_3, w_pw2_3, b_pw2_3, w_out_3,
        norm_mix_post_3, norm_mlp_pre_3, w_ff1_3, w_ff2_3, norm_mlp_post_3,
    )


_drawn_inputs = setup_inputs


def setup_inputs(seed=0):
    import zlib

    import numpy as np

    out = dict(_drawn_inputs(seed))
    spreads = {}
    factors = {}
    for name, (base, spread) in spreads.items():
        noise = np.random.default_rng([zlib.crc32(name.encode()), seed]).standard_normal(out[name].shape)
        drawn = base * np.exp(spread * noise) if base else spread * noise
        out[name] = jnp.asarray(drawn.astype(out[name].dtype))
    for name, factor in factors.items():
        out[name] = (out[name] * factor).astype(out[name].dtype)
    return out
```

```python
from contextlib import ExitStack

import numpy as np
import concourse.bass as bass
from concourse import mybir

F32 = mybir.dt.float32
U32 = mybir.dt.uint32
I32 = mybir.dt.int32
ALU = mybir.AluOpType
ACT = mybir.ActivationFunctionType
AX = mybir.AxisListType

P = 128
D = 1024
T = 512
TC = 256
KD = D // P
TT = T // P
HEADS1 = 4
CHUNK1 = 32
NCHUNK1 = T // CHUNK1
GRID_W = 64
EXPERTS = 16
CAP = 2 * T // EXPERTS
DFF1 = 2 * D
SLOTS = EXPERTS * CAP
HEADS2 = 6
PAIRS2 = HEADS2 // 2
NFF2 = 22
HEADS3 = 8
TAPS3 = 31
NFF3 = 32
INV_LEVELS = 7

WT = 32
RING = 3
EXP_CHUNKS = 3 * D * DFF1 // (P * P * WT)

PRODUCTS = [
    ("ada", 48, 8, 0),
    ("win1", 32, 8, 44),
    ("wout1", 8, 8, 8),
    ("tok1", 0, 0, 8),
    ("gather", 0, 0, 16),
    ("experts", EXPERTS * EXP_CHUNKS * WT, 1, 0),
    ("combine", 0, 0, 8),
    ("win2", 24, 8, 24),
    ("lora2", 0, 0, 6),
    ("gate2", 0, 0, 3),
    ("wout2", 8, 8, 8),
    ("ffin2", 2 * NFF2, 8, 2 * NFF2),
    ("ffout2", 8, NFF2, 8),
    ("win3a", 8, 8, 8),
    ("uqkv3", 68, 1, 28),
    ("wo3", 8, 8, 8),
    ("win3b", 30, 8, 30),
    ("pw3", 8, 8, 8),
    ("wout3", 8, 8, 8),
    ("ff1_3", 32, 8, 32),
    ("ff2_3", 8, 32, 8),
]
ARENA = 53
ORDER1 = [*range(20, 32), *range(4, 16), *range(4), *range(16, 20)]
CHUNK0, BANK0 = {}, {}
_c = _b = 0
for _name, _f, _k, _banks in PRODUCTS:
    CHUNK0[_name], BANK0[_name] = _c, _b
    _c += -(-_f * _k // WT)
    _b += _banks
NCHUNKS = _c

VECTORS = [
    ("c2", 16), ("b_ada", 48), ("norm_mix", 8), ("norm_ffn", 8), ("norm_final", 8), ("lb", 16),
    ("hg_norm", 1), ("conv1", 12), ("w_router", 128),
    ("pre_mix", 8), ("mu", 11), ("w0", 3), ("a0", 3), ("k_k", 3), ("k_a", 3), ("r_k", 3),
    ("lnx_g", 3), ("lnx_b", 3), ("ln_g", 2), ("ln_b", 2), ("post_mix", 8), ("pre_ffn", 8),
    ("post_ffn", 8), ("w2a2", 384), ("g2", 384), ("ws", 512), ("bs", 256),
    ("mix_pre3", 8), ("q_norm", 3), ("kv_norm", 2), ("conv3", 248), ("conv_b", 8), ("ln3_g", 8),
    ("ln3_b", 8), ("b_pw2", 8), ("mix_post3", 8), ("mlp_pre3", 8), ("mlp_post3", 8),
]
CONSTANTS = [
    ("ident", 128), ("ones", 128), ("ones64", 128), ("le", 128), ("lt", 128), ("future", 128),
    ("swap", 128), ("eps", 4), ("invf", 1), ("sgn", 1),
    ("blk_le", 128), ("blk_ge", 128), ("iota", 512), ("reset", 512), ("tok", 4), ("own16", 16),
    ("vblk", 4), ("onerow", 512),
]


def offsets(parts):
    at, out = 0, {}
    for name, n in parts:
        out[name] = (at, n)
        at += n
    return out, at


VOFF, NV = offsets(VECTORS)
COFF, NC = offsets(CONSTANTS)


class Semaphores:

    def __init__(self, nc, stack):
        self.nc, self.stack, self.known, self.seen = nc, stack, {}, {}

    def __getitem__(self, name):
        if name not in self.known:
            self.known[name] = self.stack.enter_context(self.nc.semaphore(name))
        return self.known[name]

    def next(self, reader, name, step=1):
        self.seen[reader, name] = self.seen.get((reader, name), 0) + step
        return self.seen[reader, name]


def three_blocks(nc, x_in, ctx_in, vec_in, const_in, levels_in, pos_in, w_in, out):
    with ExitStack() as stack:
        S = Semaphores(nc, stack)
        sb = lambda name, shape, dt=F32: stack.enter_context(nc.sbuf_tensor(name, shape, dt))
        ring = sb("ring", [P, RING, WT, P])
        X = sb("X", [P, KD, T])
        H = sb("H", [P, KD, T])
        A = sb("A", [P, ARENA, T])
        vec = sb("vec", [P, NV])
        con = sb("con", [P, NC])
        small = sb("small", [P, 512])
        PS = stack.enter_context(nc.psum_tensor("PS", [P, 8, T], F32))

        def vcol(name, j, n=1):
            return vec[:, VOFF[name][0] + j:VOFF[name][0] + j + n]

        def ccol(name, j=0, n=1):
            return con[:, COFF[name][0] + j:COFF[name][0] + j + n]

        ident, ones, ones64 = ccol("ident", 0, P), ccol("ones", 0, P), ccol("ones64", 0, P)
        eps = ccol("eps", 0)
        MOD = small[:, 0:96].rearrange("p (m w) -> p m w", w=2)
        GM = small[:, 96:112].rearrange("p (k w) -> p k w", w=2)
        GF = small[:, 112:120]
        LB, OMLB = small[:, 120:128], small[:, 128:136]
        SILU_C = small[:, 136:152].rearrange("p (k w) -> p k w", w=2)
        DEC = small[:, 152:184].rearrange("p (b n) -> p b n", n=NCHUNK1)
        LBD = small[:, 184:192]
        SMX = small[:, 192:204].rearrange("p (a t) -> p a t", t=TT)
        AFF = small[:, 256:320].rearrange("p (t e) -> p t e", e=EXPERTS)
        ICOL, GCOL = small[:, 204:212], small[:, 212:220]
        TOPV, TOPI = small[0:16, 320:384], small[0:16, 384:448]
        TOPU = small[:, 448:512].bitcast(U32)[0:16, :]

        def drained(eng, name, f):
            g = BANK0[name] + f
            eng.wait_ge(S[f"drained{g % 4}"], g // 4 + 1)

        def all_drained(eng, name, banks):
            for f in range(max(0, banks - 4), banks):
                drained(eng, name, f)

        def product_ready(eng, name, f):
            g = BANK0[name] + f
            eng.wait_ge(S["product"], g + 1)
            return PS[:, g % 4, :], S[f"drained{g % 4}"]

        def open_bank(name, f):
            g = BANK0[name] + f
            if g >= 4:
                nc.tensor.wait_ge(S[f"drained{g % 4}"], bank_uses(name, f))
            return PS[:, g % 4, :]

        def bank_uses(name, f):
            return (BANK0[name] + f) // 4

        def weight_tile(name, n, wide=1):
            g = CHUNK0[name] + n // WT
            if n % WT == 0:
                nc.tensor.wait_ge(S[f"loaded{g % RING}"], 16 * (g // RING + 1))
            v = ring[:, g % RING, n % WT:n % WT + wide, :]
            return v.rearrange("p a b -> p (a b)") if wide > 1 else v[:, 0, :]

        def products(name, fs, k_tiles, moving, out_width=T, tile0=0):
            begun = False
            for f in fs:
                bank = open_bank(name, f)
                for k in range(k_tiles):
                    n = tile0 + (f - fs[0]) * k_tiles + k
                    mm = nc.tensor.matmul(bank[:, 0:out_width], weight_tile(name, n), moving(k),
                                          start=k == 0, stop=k == k_tiles - 1)
                    begun = begun or n % WT == 0
                    if begun and k < k_tiles - 1:
                        mm.then_inc(S["chunk_used"], 1)
                        begun = False
                mm.then_inc(S["product"], 1)

        def products_loop(name, moving, rounds, k_tiles=8):
            per = WT // k_tiles
            assert (RING * per) % 4 == 0 or rounds == 1
            with nc.tensor.Fori(0, rounds) as i:
                for s in range(RING):
                    g = CHUNK0[name] + s
                    nc.tensor.wait_ge(S[f"loaded{g % RING}"], i * 16 + 16 * (g // RING + 1))
                    for j in range(per):
                        f = s * per + j
                        b = (BANK0[name] + f) % 4
                        nc.tensor.wait_ge(S[f"drained{b}"], i * (RING * per // 4) + bank_uses(name, f))
                        for k in range(k_tiles):
                            mm = nc.tensor.matmul(PS[:, b, :], ring[:, g % RING, j * k_tiles + k, :], moving(k),
                                                  start=k == 0, stop=k == k_tiles - 1)
                            if j == k == 0:
                                mm.then_inc(S["chunk_used"], 1)
                        mm.then_inc(S["product"], 1)

        def linear(name, moving):
            _, nf, _, _ = next(p for p in PRODUCTS if p[0] == name)
            per_round = RING * WT // 8
            rounds = nf // per_round
            if rounds > 1:
                products_loop(name, moving, rounds)
                rest = range(rounds * per_round, nf)
                products(name, rest, 8, moving, tile0=rounds * per_round * 8)
            else:
                products(name, range(nf), 8, moving)

        def link(eng, engine, ins):
            ins.then_inc(S[f"{engine}_step"], 1)
            eng.wait_ge(S[f"{engine}_step"], S.next(engine, f"{engine}_step"))

        def norm_squares(act, src, sq, n):
            for k in range(n):
                nc.scalar.activation(sq(k), src(k), ACT.Square).then_inc(S["squared"], 1)

        def norm_sum(pe, sq, n, bank, stat=None):
            for k in range(n):
                pe.wait_ge(S["squared"], S.next("pe", "squared"))
                mm = nc.tensor.matmul(bank, ones if stat is None else stat, sq(k), start=k == 0, stop=k == n - 1)
            mm.then_inc(S["summed"], 1)

        def norm_power(act, bank, r, width, eps_col=None, scale=None):
            act.wait_ge(S["summed"], S.next("act", "summed"))
            link(act, "act", nc.scalar.activation(r, bank, ACT.Ln, bias=eps if eps_col is None else eps_col,
                                                  scale=1.0 / width))
            nc.scalar.activation(r, r, ACT.Exp, scale=-0.5).then_inc(S["rstd"], 1)

        a = lambda n: A[:, n, :]
        Q, GB, ZF, I1, G1, GC, V1 = 0, 4, 8, 16, 20, 24, 28
        CZ = A[:, 32:38, :].rearrange("p a t -> p (a t)")
        HC = A[:, 38:42, :].rearrange("p a t -> p (a t)").rearrange("p (k t) -> p k t", t=TC)
        CX = A[:, 42:46, :].rearrange("p a t -> p (a t)").rearrange("p (k t) -> p k t", t=TC)
        MROW = lambda n: A[:, n // 2, (n % 2) * 2 * P:(n % 2 + 1) * 2 * P]
        RX, RC = a(46), A[:, 47, 0:TC]
        WIN1 = [(f, w) for f in ORDER1 for w in ((0, 1) if 4 <= f < 16 else (0,))]
        on_act = lambda f: f < 12 or 16 <= f < 20
        dest1 = lambda f: f + 4 if 4 <= f < 20 else f - 16 if 20 <= f < 24 else f
        CST = a(39), a(40)
        cstate = lambda h, d: CST[d][:, h * P:(h + 1) * P]
        CF = A[:, 24:28, :].rearrange("p a t -> p (a t)")
        CL = A[:, 28:32, :].rearrange("p a t -> p (a t)")
        CKEY = CZ[:, 0:8 * TC]
        CVAL = CZ[:, 8 * TC:12 * TC]

        def first_sync(sp):
            sp.dma_start(vec[:, :], vec_in).then_inc(S["inputs"], 16)
            sp.dma_start(con[:, :], const_in).then_inc(S["inputs"], 16)
            sp.dma_start(X[:, :, :], x_in).then_inc(S["inputs"], 16)
            sp.dma_start(CX, ctx_in).then_inc(S["inputs"], 16)
            for g in range(RING):
                sp.dma_start(ring[:, g, :, :], w_in[g].rearrange("p (a b) -> p a b", b=P)).then_inc(S[f"loaded{g}"], 16)
            rounds = NCHUNKS // RING - 1
            with sp.Fori(0, rounds) as i:
                for s in range(RING):
                    sp.wait_ge(S["chunk_used"], i * RING + s + 2)
                    sp.dma_start(ring[:, s, :, :], w_in[i * RING + (RING + s)].rearrange("p (a b) -> p a b", b=P)
                                 ).then_inc(S[f"loaded{s}"], 16)
            for g in range((rounds + 1) * RING, NCHUNKS):
                sp.wait_ge(S["chunk_used"], g - RING + 2)
                sp.dma_start(ring[:, g % RING, :, :], w_in[g].rearrange("p (a b) -> p a b", b=P)
                             ).then_inc(S[f"loaded{g % RING}"], 16)

        def first_tensor(pe):
            norm_sum(pe, lambda k: H[:, k, :], 8, PS[:, 5, :])
            norm_sum(pe, lambda k: HC[:, k, :], 8, PS[:, 6, 0:TC])
            def ada_turn(n):
                pe.wait_ge(S["ada_rows"], n + 1)
                for half in range(2):
                    rows = slice(64 * half, 64 * half + 2)
                    for f in range(2):
                        mm = nc.tensor.matmul(PS[:, (4, 7)[half], 4 * n + 2 * f:4 * n + 2 * f + 2],
                                              MROW(n)[rows, f * P:(f + 1) * P], ident[rows, rows], start=True, stop=True)
                mm.then_inc(S["ada_turned"], 1)

            pe.wait_ge(S["silu_c"], 1)
            for n in range(12):
                if n >= 2:
                    pe.wait_ge(S["ada_rows"], n - 1)
                for k in range(8):
                    for half in range(2):
                        mm = nc.tensor.matmul(PS[64 * half:64 * half + 2, 2 * (n % 2) + half, 0:2 * P], SILU_C[:, k, :],
                                              weight_tile("ada", n * WT + 4 * k + 2 * half, 2), start=k == 0, stop=k == 7)
                        if k == half == 0:
                            mm.then_inc(S["chunk_used"], 1)
                mm.then_inc(S["ada"], 1)
                if n:
                    ada_turn(n - 1)
            ada_turn(11)
            pe.wait_ge(S["h_ready"], S.next("pe", "h_ready", 2))
            e = 0
            for n, f in enumerate(ORDER1):
                both = 4 <= f < 16
                bank = open_bank("win1", e)
                bank_c = open_bank("win1", e + 1) if both else None
                for k in range(8):
                    w = weight_tile("win1", n * 8 + k)
                    mm = nc.tensor.matmul(bank, w, H[:, k, :], start=k == 0, stop=k == 7)
                    if (n * 8 + k) % WT == 0:
                        mm.then_inc(S["chunk_used"], 1)
                    if k == 7:
                        mm.then_inc(S["product"], 1)
                    if both:
                        mc = nc.tensor.matmul(bank_c[:, 0:TC], w, HC[:, k, :], start=k == 0, stop=k == 7)
                if both:
                    mc.then_inc(S["product"], 1)
                e += 2 if both else 1
            pe.wait_ge(S["ckeys"], 1)

            def context_tokens(u):
                h, d = u // 2, u % 2
                if u >= 2:
                    pe.wait_ge(S["ctok_out"], u - 1)
                for tt in range(2):
                    nc.tensor.transpose(PS[:, 4 + u % 2, tt * P:(tt + 1) * P],
                                        CF[:, (4 * d + h) * TC + tt * P:(4 * d + h) * TC + (tt + 1) * P], ident)
                    mm = nc.tensor.transpose(PS[:, 4 + u % 2, (2 + tt) * P:(3 + tt) * P],
                                             CVAL[:, h * TC + tt * P:h * TC + (tt + 1) * P], ident)
                mm.then_inc(S["ctok"], 1)

            context_tokens(0)
            for u in range(8):
                if u < 7:
                    context_tokens(u + 1)
                pe.wait_ge(S["ctok_out"], u + 1)
                if u >= 2:
                    pe.wait_ge(S["cstate"], u - 1)
                for tt in range(2):
                    mm = nc.tensor.matmul(PS[:, 6 + u % 2, 0:P], CTOK[u % 2][:, tt * P:(tt + 1) * P],
                                          CTOK[u % 2][:, (2 + tt) * P:(3 + tt) * P], start=tt == 0, stop=tt == 1)
                mm.then_inc(S["ckv"], 1)
            linear_attention_tensor(pe)
            pe.wait_ge(S["mixed1"], HEADS1)
            pe.wait_ge(S["conv1"], 4)
            products("wout1", range(8), 8, lambda k: A[:, k, :])
            norm_sum(pe, lambda k: H[:, k, :], 8, PS[:, 5, :])
            pe.wait_ge(S["h_ready"], S.next("pe", "h_ready"))
            for tt in range(TT):
                for k in range(8):
                    mm = nc.tensor.matmul(PS[:, 6, tt * EXPERTS:(tt + 1) * EXPERTS], H[:, k, tt * P:(tt + 1) * P],
                                          vcol("w_router", k * EXPERTS, EXPERTS), start=k == 0, stop=k == 7)
            mm.then_inc(S["logits"], 1)
            for k in range(8):
                bank = open_bank("tok1", k)
                for tt in range(TT):
                    mm = nc.tensor.transpose(bank[:, tt * P:(tt + 1) * P], H[:, k, tt * P:(tt + 1) * P], ident)
                mm.then_inc(S["product"], 1)
            pe.wait_ge(S["aff"], 1)
            for tt in range(TT):
                mm = nc.tensor.transpose(PS[0:EXPERTS, 7, tt * P:(tt + 1) * P], AFF[:, tt, :], ident)
            mm.then_inc(S["aff_t"], 1)
            pe.wait_ge(S["top"], 1)
            nc.tensor.transpose(PS[0:CAP, 7, 0:EXPERTS], TOPI, ident[0:EXPERTS, 0:EXPERTS])
            nc.tensor.transpose(PS[0:CAP, 7, 64:64 + EXPERTS], TOPV, ident[0:EXPERTS, 0:EXPERTS]).then_inc(S["top_t"], 1)
            for half in range(2):
                mm = nc.tensor.matmul(PS[:, 4 + half, :], ones[0:EXPERTS, :], IDXROW[:, half * T:(half + 1) * T],
                                      start=True, stop=True)
            mm.then_inc(S["idx"], 1)
            pe.wait_ge(S["pick"], 1)
            all_drained(pe, "tok1", 8)
            for k in range(8):
                for half in range(2):
                    bank = open_bank("gather", 2 * k + half)
                    for tt in range(TT):
                        mm = nc.tensor.matmul(bank, HTOK[:, tt, k * P:(k + 1) * P],
                                              PICK[:, tt, half * T:(half + 1) * T], start=tt == 0, stop=tt == TT - 1)
                    mm.then_inc(S["product"], 1)
            all_drained(pe, "gather", 16)
            experts_tensor(pe)
            pe.wait_ge(S["y_out"], EXPERTS + 1)
            for k in range(8):
                bank = open_bank("combine", k)
                for j in range(8):
                    mm = nc.tensor.matmul(bank, YS[:, j, k * P:(k + 1) * P], PUT[:, j, :], start=j == 0, stop=j == 7)
                mm.then_inc(S["product"], 1)
            norm_sum(pe, lambda k: H[:, k, :], 8, PS[:, 5, :])

        TF, LF, PR, CU, RE = a(32), a(33), a(34), a(35), a(36)
        TK = (a(37), a(38))
        QD = (a(41), a(42), a(43), a(44))
        KI = (a(45), a(46))
        KE = (a(47), a(48))
        KET = (a(49), a(50))
        SC = lambda h, d: a(ZF + 4 * d + h)
        VT = lambda h: a(I1 + h)
        VB = A[:, 24:28, :]
        RO, OO = a(30), a(31)
        ST = (H[:, 0:4, :].rearrange("p a t -> p (a t)"), H[:, 4:8, :].rearrange("p a t -> p (a t)"))
        CTOK = (a(51), a(52))

        def linear_attention_tensor(pe):
            all_drained(pe, "win1", 44)
            pe.wait_ge(S["cstate"], 8)

            def values(h):
                if h:
                    pe.wait_ge(S["vtok"], h)
                for tt in range(TT):
                    mm = nc.tensor.transpose(PS[:, 5, tt * P:(tt + 1) * P], A[:, I1 + h, tt * P:(tt + 1) * P], ident)
                mm.then_inc(S["v_t"], 1)

            def keys_scores(u):
                pe.wait_ge(S["qk"], u + 1)
                if u:
                    pe.wait_ge(S["ke_tok"], u)
                for tt in range(TT):
                    mm = nc.tensor.transpose(PS[:, 6, tt * P:(tt + 1) * P], KE[u % 2][:, tt * P:(tt + 1) * P], ident)
                mm.then_inc(S["ke_t"], 1)
                if u:
                    pe.wait_ge(S["scores_out"], u)
                for tt in range(TT):
                    s = slice(tt * P, (tt + 1) * P)
                    mm = nc.tensor.matmul(PS[:, 7, s], KI[u % 2][:, s], QD[u % 4][:, s], start=True, stop=True)
                mm.then_inc(S["scores"], 1)

            def keys_values(u):
                h, d = u // 2, u % 2
                pe.wait_ge(S["ke_tok"], u + 1)
                pe.wait_ge(S["vblock"], h + 1)
                for n, tt in enumerate(range(TT) if d == 0 else reversed(range(TT))):
                    if u or n > 1:
                        pe.wait_ge(S["kv_used"], 4 * u + n - 1)
                    nc.tensor.matmul(PS[:, (4, 3)[n % 2], :], KET[u % 2][:, tt * P:(tt + 1) * P], VB[:, tt, :],
                                     start=True, stop=True).then_inc(S["kv"], 1)

            def outputs(h, tiles):
                for tt in tiles:
                    o = PS[:, 0, tt * P:(tt + 1) * P]
                    for d in range(2):
                        nc.tensor.matmul(o, VT(h)[:, tt * P:(tt + 1) * P], SC(h, d)[:, tt * P:(tt + 1) * P],
                                         start=d == 0, stop=d == 1)
                    for c in range(4):
                        n = 4 * tt + c
                        for d in range(2):
                            mm = nc.tensor.matmul(PS[:, 0, n * CHUNK1:(n + 1) * CHUNK1], ST[d][:, n * P:(n + 1) * P],
                                                  QD[(2 * h + d) % 4][:, n * CHUNK1:(n + 1) * CHUNK1],
                                                  start=False, stop=True, skip_group_check=True)
                return mm

            values(0)
            keys_scores(0)
            for h in range(HEADS1):
                keys_values(2 * h)
                keys_scores(2 * h + 1)
                if h:
                    norm_sum(pe, lambda k: OO, 1, PS[:, 1, :])
                keys_values(2 * h + 1)
                if h:
                    pe.wait_ge(S["mixed1"], h)
                pe.wait_ge(S["vtok"], h + 1)
                pe.wait_ge(S["scores_out"], 2 * h + 2)
                pe.wait_ge(S["kv_used"], 8 * h + 8)
                outputs(h, range(2))
                if h + 1 < HEADS1:
                    values(h + 1)
                    keys_scores(2 * h + 2)
                outputs(h, range(2, TT)).then_inc(S["o"], 1)
            norm_sum(pe, lambda k: OO, 1, PS[:, 1, :])

        def log_act(act, u):
            act.wait_ge(S["gate"], u + 1)
            nc.scalar.activation(LF, TF, ACT.Ln).then_inc(S["logf"], 1)

        def decays_act(act, u):
            act.wait_ge(S["cum"], u + 1)
            if u >= 2:
                act.wait_ge(S["kv_used"], 4 * u - 4)
            if u >= 4:
                act.wait_ge(S["o"], u // 2 - 1)
            nc.scalar.activation(QD[u % 4], CU, ACT.Exp)
            nc.scalar.activation(KI[u % 2], CU, ACT.Exp, scale=-1.0)
            nc.scalar.activation(KE[u % 2], RE, ACT.Exp)
            nc.scalar.activation(DEC[:, u % 2, :], TOTAL[u % 2], ACT.Exp).then_inc(S["exps"], 1)

        TOTAL = (small[:, 220:236], small[:, 236:252])

        def linear_attention_act(act):
            def keys_turned(u):
                act.wait_ge(S["ke_t"], u + 1)
                if u >= 2:
                    act.wait_ge(S["kv"], 4 * u - 4)
                nc.scalar.activation(KET[u % 2], PS[:, 6, :], ACT.Copy).then_inc(S["ke_tok"], 1)

            def output_square(h):
                act.wait_ge(S["o"], h + 1)
                nc.scalar.activation(OO, PS[:, 0, :], ACT.Square).then_inc(S["squared"], 1)

            log_act(act, 0)
            decays_act(act, 0)
            for h in range(HEADS1):
                log_act(act, 2 * h + 1)
                keys_turned(2 * h)
                decays_act(act, 2 * h + 1)
                if h:
                    output_square(h - 1)
                keys_turned(2 * h + 1)
                if h:
                    norm_power(act, PS[:, 1, :], RO, P)
                if h + 1 < HEADS1:
                    log_act(act, 2 * h + 2)
                    decays_act(act, 2 * h + 2)
            output_square(HEADS1 - 1)
            norm_power(act, PS[:, 1, :], RO, P)

        def gates_dve(dve, u):
            h, d = u // 2, u % 2
            if u:
                dve.wait_ge(S["exps"], u)
            b = 4 * d + h
            link(dve, "dve", nc.vector.tensor_scalar(TF, a(ZF + b), OMLB[:, b:b + 1], LB[:, b:b + 1], ALU.mult, ALU.add))
            nc.vector.tensor_scalar(TK[u % 2], TF, -1.0, 1.0, ALU.mult, ALU.add).then_inc(S["gate"], 1)

        def running_sums_dve(dve, u):
            dve.wait_ge(S["logf"], u + 1)
            link(dve, "dve", nc.vector.tensor_tensor_scan(PR, ccol("reset", 0, T), LF, 0.0, ALU.mult, ALU.add))
            r = lambda t: t.rearrange("p (n c) -> p n c", c=CHUNK1)
            tot = r(PR)[:, :, CHUNK1 - 1:CHUNK1]
            link(dve, "dve", nc.vector.tensor_copy(TOTAL[u % 2].rearrange("p (n c) -> p n c", c=1), tot))
            tot = tot.to_broadcast([P, NCHUNK1, CHUNK1])
            if u % 2 == 0:
                nc.vector.tensor_copy(CU, PR)
                link(dve, "dve", nc.vector.tensor_tensor(r(RE), tot, r(PR), ALU.subtract))
            else:
                link(dve, "dve", nc.vector.tensor_tensor(RE, PR, LF, ALU.subtract))
                link(dve, "dve", nc.vector.tensor_tensor(r(CU), tot, r(RE), ALU.subtract))
            dve.sem_inc(S["cum"], 1)

        def decayed_dve(dve, u):
            dve.wait_ge(S["exps"], u + 1)
            nc.vector.tensor_tensor(QD[u % 4], a(Q + u // 2), QD[u % 4], ALU.mult)
            nc.vector.tensor_tensor(KI[u % 2], TK[u % 2], KI[u % 2], ALU.mult)
            nc.vector.tensor_tensor(KE[u % 2], TK[u % 2], KE[u % 2], ALU.mult).then_inc(S["qk"], 1)

        def linear_attention_dve(dve):
            def masked_scores(u):
                dve.wait_ge(S["scores"], u + 1)
                mask = ccol("blk_le" if u % 2 == 0 else "blk_ge", 0, P).unsqueeze(1).to_broadcast([P, TT, P])
                t4 = lambda v: v.rearrange("p (a b) -> p a b", b=P)
                nc.vector.tensor_tensor(t4(SC(u // 2, u % 2)), t4(PS[:, 7, :]), mask, ALU.mult).then_inc(S["scores_out"], 1)

            def states(u):
                h, d = u // 2, u % 2
                order = list(range(NCHUNK1)) if d == 0 else list(reversed(range(NCHUNK1)))
                s = lambda n: ST[d][:, n * P:(n + 1) * P]
                if h:
                    dve.wait_ge(S["o"], h)
                link(dve, "dve", nc.vector.tensor_copy(s(order[0]), cstate(h, d)))
                for m, n in enumerate(order):
                    if m % 4 == 0:
                        dve.wait_ge(S["kv"], 4 * u + m // 4 + 1)
                    bank = PS[:, (4, 3)[(m // 4) % 2], :]
                    c = n % 4
                    if m < NCHUNK1 - 1:
                        v = nc.vector.scalar_tensor_tensor(s(order[m + 1]), s(n), DEC[:, u % 2, n:n + 1],
                                                           bank[:, c * P:(c + 1) * P], ALU.mult, ALU.add)
                        if m % 4 == 3:
                            v.then_inc(S["kv_used"], 1)
                            dve.wait_ge(S["kv_used"], 4 * u + m // 4 + 1)
                        else:
                            link(dve, "dve", v)
                    else:
                        dve.sem_inc(S["kv_used"], 1)

            def normed_output(h):
                dve.wait_ge(S["rstd"], S.next("dve", "rstd"))
                link(dve, "dve", nc.vector.scalar_tensor_tensor(RO, PS[:, 0, :], vcol("hg_norm", 0), RO, ALU.mult, ALU.mult))
                nc.vector.tensor_tensor(a(Q + h), RO, a(G1 + h), ALU.mult).then_inc(S["mixed1"], 1)

            gates_dve(dve, 0)
            running_sums_dve(dve, 0)
            decayed_dve(dve, 0)
            for h in range(HEADS1):
                dve.wait_ge(S["v_t"], h + 1)
                nc.vector.tensor_copy(VT(h), PS[:, 5, :]).then_inc(S["vtok"], 1)
                gates_dve(dve, 2 * h + 1)
                dve.wait_ge(S["vtok"], h + 1)
                for tt in range(TT):
                    for c in range(4):
                        v = nc.vector.tensor_scalar(VB[:, tt, c * P:(c + 1) * P], VT(h)[:, tt * P:(tt + 1) * P],
                                                    ccol("vblk", c), None, ALU.mult)
                v.then_inc(S["vblock"], 1)
                running_sums_dve(dve, 2 * h + 1)
                masked_scores(2 * h)
                decayed_dve(dve, 2 * h + 1)
                states(2 * h)
                if h:
                    normed_output(h - 1)
                if h + 1 < HEADS1:
                    gates_dve(dve, 2 * h + 2)
                masked_scores(2 * h + 1)
                if h + 1 < HEADS1:
                    running_sums_dve(dve, 2 * h + 2)
                states(2 * h + 1)
                if h + 1 < HEADS1:
                    decayed_dve(dve, 2 * h + 2)
            normed_output(HEADS1 - 1)

        HTOK = A[:, 0:8, :].rearrange("p (a b) t -> p a (b t)", a=TT)
        PICK = A[:, 8:16, :].rearrange("p (a b) t -> p a (b t)", a=TT)
        YS = A[:, 0:16, :].rearrange("p (a b) t -> p a (b t)", a=8)
        XS = A[:, 16:32, :].rearrange("p (a b) t -> p a (b t)", a=8)
        PUT = A[:, 32:40, :]
        XE = [A[:, 40 + b, :].rearrange("p (k s) -> p k s", s=CAP) for b in range(2)]
        SG = [A[CAP:P, 42 + b, :] for b in range(2)]
        HID = A[0:CAP, 44:48, :]
        HT = A[:, 48:50, :].rearrange("p a t -> p (a t)").rearrange("p (k s) -> p k s", s=CAP)
        AFT = (A[0:EXPERTS, 50, :], A[0:EXPERTS, 51, :])
        IDXROW = A[0:EXPERTS, 44:46, :].rearrange("p a t -> p (a t)")

        def experts_tensor(pe):
            pe.sem_inc(S["hid_turned"], 4)
            pe.sem_inc(S["gate_up"], 8)
            pe.sem_inc(S["y"], 1)
            g0 = CHUNK0["experts"]
            with pe.Fori(0, EXPERTS // 2) as i:
                for b in range(2):
                    at = lambda per, n: i * (2 * per) + (b * per + n)
                    chunk = [12 * b]

                    def arrive():
                        n = chunk[0]
                        g = g0 + n
                        pe.wait_ge(S[f"loaded{g % RING}"], i * (24 // RING * 16) + 16 * (g // RING + 1))
                        chunk[0] += 1
                        return ring[:, g % RING, :, :]

                    def turn(c):
                        pe.wait_ge(S["hid"], at(4, c + 3))
                        pe.wait_ge(S["turned_out"], at(4, c + 1))
                        for j in range(4):
                            mm = nc.tensor.matmul(PS[:, 4 + c % 2, j * CAP:(j + 1) * CAP],
                                                  HID[:, c, j * P:(j + 1) * P], ident[0:CAP, 0:CAP],
                                                  start=True, stop=True)
                        mm.then_inc(S["hid_turned"], 1)

                    def down(c):
                        w = arrive()
                        pe.wait_ge(S["turned_out"], at(4, c + 3))
                        if c == 0:
                            pe.wait_ge(S["y_out"], at(1, 1))
                        for j in range(4):
                            for half in range(2):
                                n = 8 * j + 4 * half
                                mm = nc.tensor.matmul(PS[CAP * half:CAP * (half + 1), 6 + half, :], HT[:, 4 * c + j, :],
                                                      w[:, n:n + 4, :].rearrange("p a b -> p (a b)"),
                                                      start=c == j == 0, stop=c == j == 3)
                                if j == half == 0:
                                    mm.then_inc(S["chunk_used"], 1)
                        return mm

                    pe.wait_ge(S["xe"], at(1, 1))
                    for c in range(4):
                        pe.wait_ge(S["silu"], at(4, c + 1))
                        pe.wait_ge(S["hid"], at(4, c + 1))
                        for k in range(8):
                            if k % 4 == 0:
                                w = arrive()
                            for up in range(2):
                                n = 8 * (k % 4) + 4 * up
                                mm = nc.tensor.matmul(PS[CAP * up:CAP * (up + 1), 2 * (c % 2) + up, :], XE[b][:, k, :],
                                                      w[:, n:n + 4, :].rearrange("p a b -> p (a b)"), start=k == 0, stop=k == 7)
                                if k % 4 == up == 0:
                                    mm.then_inc(S["chunk_used"], 1)
                        mm.then_inc(S["gate_up"], 1)
                        if c:
                            turn(c - 1)
                    down(0)
                    turn(3)
                    down(1)
                    down(2)
                    down(3).then_inc(S["y"], 1)

        def experts_act(act):
            act.sem_inc(S["silu"], 2)
            act.sem_inc(S["turned_out"], 2)
            with act.Fori(0, EXPERTS // 2) as i:
                for b in range(2):
                    at = lambda per, n: i * (2 * per) + (b * per + n)

                    def turned(c):
                        act.wait_ge(S["hid_turned"], at(4, c + 5))
                        if c == 0:
                            act.wait_ge(S["y"], at(1, 1))
                        nc.scalar.activation(HT[:, 4 * c:4 * c + 4, :].rearrange("p a b -> p (a b)"),
                                             PS[:, 4 + c % 2, 0:4 * CAP], ACT.Copy).then_inc(S["turned_out"], 1)

                    for c in range(4):
                        act.wait_ge(S["gate_up"], at(4, c + 9))
                        act.wait_ge(S["hid"], at(4, c + 1))
                        nc.scalar.activation(SG[c % 2], PS[0:CAP, 2 * (c % 2), :], ACT.Silu).then_inc(S["silu"], 1)
                        if c:
                            turned(c - 1)
                    turned(3)

        def experts_dve(dve):
            dve.sem_inc(S["hid"], 2)
            dve.sem_inc(S["y_out"], 1)
            with dve.Fori(0, EXPERTS // 2) as i:
                for b in range(2):
                    at = lambda per, n: i * (2 * per) + (b * per + n)
                    for c in range(4):
                        dve.wait_ge(S["silu"], at(4, c + 3))
                        dve.wait_ge(S["hid_turned"], at(4, c + 1))
                        nc.vector.tensor_tensor(HID[:, c, :], SG[c % 2], PS[CAP:P, 2 * (c % 2) + 1, :],
                                                ALU.mult).then_inc(S["hid"], 1)
                    dve.wait_ge(S["y"], at(1, 2))
                    for half in range(2):
                        v = nc.vector.tensor_copy(YS[CAP * b:CAP * (b + 1), bass.ds(i, 1), half * T:(half + 1) * T],
                                                  PS[CAP * half:CAP * (half + 1), 6 + half, :].unsqueeze(1))
                    v.then_inc(S["y_out"], 1)

        def experts_pool(pool):
            all_drained(pool, "gather", 16)
            with pool.Fori(0, EXPERTS // 2) as i:
                for b in range(2):
                    pool.wait_ge(S["gate_up"], i * 8 + 4 * b + 4)
                    nc.gpsimd.tensor_copy(XE[b], XS[:, :, bass.ds(i * (2 * CAP) + b * CAP, CAP)]).then_inc(S["xe"], 1)

        def first_act(act):
            act.wait_ge(S["inputs"], 64)
            nc.scalar.activation(SILU_C.rearrange("p a b -> p (a b)"), vcol("c2", 0, 16), ACT.Silu).then_inc(S["silu_c"], 1)
            norm_squares(act, lambda k: X[:, k, :], lambda k: H[:, k, :], 8)
            norm_squares(act, lambda k: CX[:, k, :], lambda k: HC[:, k, :], 8)
            norm_power(act, PS[:, 5, :], RX, D)
            norm_power(act, PS[:, 6, 0:TC], RC, D)
            act.wait_ge(S["lb_diff"], 1)
            link(act, "act", nc.scalar.activation(LB, LBD, ACT.Sigmoid))
            nc.scalar.activation(OMLB, LB, ACT.Identity, scale=-1.0, bias=ccol("ones", 0)).then_inc(S["lb"], 1)
            for e, (f, w) in enumerate(WIN1):
                if on_act(f):
                    bank, done = product_ready(act, "win1", e)
                    func = ACT.Copy if f < 4 else ACT.Silu if f >= 16 else ACT.Sigmoid
                    dst = CZ[:, (f - 4) * TC:(f - 3) * TC] if w else a(dest1(f))
                    nc.scalar.activation(dst, bank[:, 0:TC] if w else bank, func).then_inc(done, 1)
                if f == 11 and w:
                    act.wait_ge(S["cgate"], 1)
                    nc.scalar.activation(CL, CF, ACT.Ln).then_inc(S["clog"], 1)
                if f == 3:
                    act.wait_ge(S["crem"], 1)
                    nc.scalar.activation(CF, CF, ACT.Exp).then_inc(S["cexp"], 1)
            for u in range(8):
                act.wait_ge(S["ctok"], u + 1)
                if u >= 2:
                    act.wait_ge(S["ckv"], u - 1)
                nc.scalar.activation(CTOK[u % 2], PS[:, 4 + u % 2, :], ACT.Copy).then_inc(S["ctok_out"], 1)
            linear_attention_act(act)
            for k in range(8):
                drained(act, "wout1", k)
                nc.scalar.activation(H[:, k, :], X[:, k, :], ACT.Square).then_inc(S["squared"], 1)
            norm_power(act, PS[:, 5, :], a(52), D)
            act.wait_ge(S["rmax"], 1)
            nc.scalar.activation(AFF.rearrange("p a b -> p (a b)"), AFF.rearrange("p a b -> p (a b)"), ACT.Exp
                                 ).then_inc(S["rexp"], 1)
            for k in range(8):
                bank, done = product_ready(act, "tok1", k)
                nc.scalar.activation(HTOK[:, :, k * P:(k + 1) * P], bank.rearrange("p (a b) -> p a b", b=P), ACT.Copy
                                     ).then_inc(done, 1)
            for f in range(16):
                bank, done = product_ready(act, "gather", f)
                nc.scalar.activation(XS[:, f // 2, (f % 2) * T:(f % 2 + 1) * T], bank, ACT.Copy).then_inc(done, 1)
            experts_act(act)
            for k in range(8):
                drained(act, "combine", k)
                nc.scalar.activation(H[:, k, :], X[:, k, :], ACT.Square).then_inc(S["squared"], 1)
            norm_power(act, PS[:, 5, :], a(52), D)

        def convolution_dve(dve):
            grid = lambda t: t.rearrange("p (r w) -> p r w", w=GRID_W)
            for k in range(4):
                u, y, z = a(GC + k), a(GB + k), a(V1 + k)
                link(dve, "dve", nc.vector.tensor_tensor(u, u, z, ALU.mult))
                link(dve, "dve", nc.vector.tensor_scalar(z, u, vcol("conv1", 4 + k), None, ALU.mult))
                link(dve, "dve", nc.vector.scalar_tensor_tensor(grid(z)[:, :, 1:], grid(u)[:, :, :-1], vcol("conv1", k),
                                                                grid(z)[:, :, 1:], ALU.mult, ALU.add))
                link(dve, "dve", nc.vector.scalar_tensor_tensor(grid(z)[:, :, :-1], grid(u)[:, :, 1:], vcol("conv1", 8 + k),
                                                                grid(z)[:, :, :-1], ALU.mult, ALU.add))
                nc.vector.tensor_tensor(y, y, z, ALU.mult).then_inc(S["conv1"], 1)

        def first_dve(dve):
            dve.wait_ge(S["inputs"], 64)
            nc.vector.tensor_tensor(LBD, vcol("lb", 0, 8), vcol("lb", 8, 8), ALU.subtract).then_inc(S["lb_diff"], 1)
            for n in range(12):
                dve.wait_ge(S["ada"], n + 1)
                for half in range(2):
                    rows = slice(64 * half, 64 * half + 2)
                    v = nc.vector.tensor_copy(MROW(n)[rows, :], PS[rows, 2 * (n % 2) + half, 0:2 * P])
                v.then_inc(S["ada_rows"], 1)
            dve.wait_ge(S["ada_turned"], 12)
            for half in range(2):
                v = nc.vector.tensor_tensor(
                    MOD.rearrange("p (n h f) w -> p n h f w", h=2, f=2)[:, :, half],
                    PS[:, (4, 7)[half], 0:48].rearrange("p (n f w) -> p n f w", f=2, w=2),
                    vcol("b_ada", 0, 48).rearrange("p (n h f) -> p n h f", h=2, f=2)[:, :, half].unsqueeze(3)
                    .to_broadcast([P, 12, 2, 2]), ALU.add)
            link(dve, "dve", v)
            for w in range(2):
                link(dve, "dve", nc.vector.scalar_tensor_tensor(GM[:, :, w], MOD[:, 8:16, w], 1.0, vcol("norm_mix", 0, 8),
                                                                ALU.add, ALU.mult))
            link(dve, "dve", nc.vector.scalar_tensor_tensor(GF, MOD[:, 32:40, 0], 1.0, vcol("norm_ffn", 0, 8), ALU.add, ALU.mult))
            for dst, src, r, w in ((H, X, RX, 0), (HC, CX, RC, 1)):
                dve.wait_ge(S["rstd"], S.next("dve", "rstd"))
                for k in range(8):
                    v = nc.vector.scalar_tensor_tensor(dst[:, k, :], src[:, k, :], GM[:, k, w:w + 1], r, ALU.mult, ALU.mult)
                link(dve, "dve", v)
                for k in range(8):
                    v = nc.vector.tensor_scalar(dst[:, k, :], dst[:, k, :], MOD[:, k, w:w + 1], None, ALU.add)
                v.then_inc(S["h_ready"], 1)
            for e, (f, w) in enumerate(WIN1):
                if not on_act(f):
                    bank, done = product_ready(dve, "win1", e)
                    dst = CZ[:, (f - 4) * TC:(f - 3) * TC] if w else a(dest1(f))
                    nc.vector.tensor_copy(dst, bank[:, 0:TC] if w else bank).then_inc(done, 1)
                if e == 11:
                    all_drained(dve, "win1", 12)
                    convolution_dve(dve)
            all_drained(dve, "win1", 36)
            dve.wait_ge(S["lb"], 1)
            c = lambda t, b: t[:, b * TC:(b + 1) * TC]
            for b in range(8):
                v = nc.vector.tensor_scalar(c(CF, b), c(CKEY, b), OMLB[:, b:b + 1], LB[:, b:b + 1], ALU.mult, ALU.add)
            link(dve, "dve", v)
            nc.vector.tensor_scalar(CKEY, CF, -1.0, 1.0, ALU.mult, ALU.add).then_inc(S["cgate"], 1)
            dve.wait_ge(S["clog"], 1)
            for b in range(8):
                v = nc.vector.tensor_tensor_scan(c(CF, b), ccol("onerow", 0, TC), c(CL, b), 0.0, ALU.mult, ALU.add)
            link(dve, "dve", v)
            for b in range(8):
                if b < 4:
                    link(dve, "dve", nc.vector.tensor_copy(DUMMYC, c(CF, b)[:, TC - 1:TC]))
                    v = nc.vector.tensor_scalar(c(CF, b), c(CF, b), DUMMYC, -1.0, ALU.subtract, ALU.mult)
                else:
                    v = nc.vector.tensor_tensor(c(CF, b), c(CF, b), c(CL, b), ALU.subtract)
                if b < 7:
                    link(dve, "dve", v)
            v.then_inc(S["crem"], 1)
            dve.wait_ge(S["cexp"], 1)
            nc.vector.tensor_tensor(CF, CF, CKEY, ALU.mult).then_inc(S["ckeys"], 1)
            for u in range(8):
                dve.wait_ge(S["ckv"], u + 1)
                nc.vector.tensor_copy(cstate(u // 2, u % 2), PS[:, 6 + u % 2, 0:P]).then_inc(S["cstate"], 1)
            dve.wait_ge(S["cstate"], 8)
            all_drained(dve, "win1", 44)
            linear_attention_dve(dve)
            for k in range(8):
                bank, done = product_ready(dve, "wout1", k)
                nc.vector.scalar_tensor_tensor(X[:, k, :], bank, MOD[:, 16 + k, 0:1], X[:, k, :], ALU.mult, ALU.add
                                               ).then_inc(done, 1)
            all_drained(dve, "wout1", 8)
            dve.wait_ge(S["rstd"], S.next("dve", "rstd"))
            for k in range(8):
                v = nc.vector.scalar_tensor_tensor(H[:, k, :], X[:, k, :], GF[:, k:k + 1], a(52), ALU.mult, ALU.mult)
            link(dve, "dve", v)
            for k in range(8):
                v = nc.vector.tensor_scalar(H[:, k, :], H[:, k, :], MOD[:, 24 + k, 0:1], None, ALU.add)
            v.then_inc(S["h_ready"], 1)
            dve.wait_ge(S["logits"], 1)
            lg = PS[:, 6, 0:TT * EXPERTS].rearrange("p (t e) -> p t e", e=EXPERTS)
            wide = lambda j: SMX[:, j, :].unsqueeze(2).to_broadcast([P, TT, EXPERTS])
            link(dve, "dve", nc.vector.tensor_reduce(SMX[:, 0, :], lg, AX.X, ALU.max))
            nc.vector.tensor_tensor(AFF, lg, wide(0), ALU.subtract).then_inc(S["rmax"], 1)
            dve.wait_ge(S["rexp"], 1)
            link(dve, "dve", nc.vector.tensor_reduce(SMX[:, 1, :], AFF, AX.X, ALU.add))
            link(dve, "dve", nc.vector.reciprocal(SMX[:, 2, :], SMX[:, 1, :]))
            nc.vector.tensor_tensor(AFF, AFF, wide(2), ALU.mult).then_inc(S["aff"], 1)
            dve.wait_ge(S["aff_t"], 1)
            link(dve, "dve", nc.vector.tensor_copy(AFT[0], PS[0:EXPERTS, 7, :]))
            for r in range(CAP // 8):
                s = slice(8 * r, 8 * r + 8)
                link(dve, "dve", nc.vector.max(TOPV[:, s], AFT[r % 2]))
                link(dve, "dve", nc.vector.max_index(TOPU[:, s], TOPV[:, s], AFT[r % 2]))
                link(dve, "dve", nc.vector.match_replace(AFT[1 - r % 2], TOPV[:, s], AFT[r % 2], -1.0))
            link(dve, "dve", nc.vector.tensor_copy(TOPI, TOPU))
            nc.vector.tensor_tensor(IDXROW.rearrange("p (e r) -> p e r", r=CAP),
                                    TOPI.unsqueeze(1).to_broadcast([EXPERTS, EXPERTS, CAP]),
                                    ccol("own16", 0, 16)[0:EXPERTS, :].unsqueeze(2).to_broadcast([EXPERTS, EXPERTS, CAP]),
                                    ALU.mult).then_inc(S["top"], 1)
            dve.wait_ge(S["top_t"], 1)
            for b in range(2):
                rows = slice(CAP * b, CAP * (b + 1))
                for col, o in ((ICOL, 0), (GCOL, 64)):
                    v = nc.vector.tensor_copy(col[rows, :], PS[0:CAP, 7, o:o + 16].rearrange("p (j b) -> p j b", b=2)[:, :, b])
            link(dve, "dve", v)
            dve.wait_ge(S["idx"], 1)
            for tt in range(TT):
                v = nc.vector.tensor_scalar(PICK[:, tt, :], PS[:, 4:6, :].rearrange("p a t -> p (a t)"), ccol("tok", tt), None,
                                            ALU.is_equal)
            v.then_inc(S["pick"], 1)
            for j in range(8):
                v = nc.vector.tensor_scalar(PUT[:, j, :], ccol("iota", 0, T), ICOL[:, j:j + 1], GCOL[:, j:j + 1],
                                            ALU.is_equal, ALU.mult)
            link(dve, "dve", v)
            experts_dve(dve)
            for k in range(8):
                bank, done = product_ready(dve, "combine", k)
                nc.vector.scalar_tensor_tensor(X[:, k, :], bank, MOD[:, 40 + k, 0:1], X[:, k, :], ALU.mult, ALU.add
                                               ).then_inc(done, 1)
            all_drained(dve, "combine", 8)
            dve.wait_ge(S["rstd"], S.next("dve", "rstd"))
            for k in range(8):
                nc.vector.scalar_tensor_tensor(X[:, k, :], X[:, k, :], vcol("norm_final", k), a(52), ALU.mult, ALU.mult
                                               ).then_inc(S["x_new"], 1)

        def first_pool(pool):
            experts_pool(pool)

        DUMMYC = small[:, 252:253]

        R2 = a(52)
        LEVELS = con[:, COFF["blk_le"][0]:COFF["blk_le"][0] + 2 * INV_LEVELS * P]
        level = lambda n, turned: LEVELS[:, (turned * INV_LEVELS + n) * P:(turned * INV_LEVELS + n + 1) * P]
        as_tiles = lambda v: v.rearrange("p (a b) -> p a b", b=P)

        def pre_norm_act(act):
            for k in range(8):
                act.wait_ge(S["x_new"], S.next("act", "x_new"))
                nc.scalar.activation(H[:, k, :], X[:, k, :], ACT.Square).then_inc(S["squared"], 1)
            norm_power(act, PS[:, 5, :], R2, D)

        def pre_norm_tensor(pe):
            norm_sum(pe, lambda k: H[:, k, :], 8, PS[:, 5, :])

        def normed_input(pe):
            base, waited = S.next("pe", "h_ready", 8) - 8, set()

            def tile(k):
                if k not in waited:
                    pe.wait_ge(S["h_ready"], base + k + 1)
                    waited.add(k)
                return H[:, k, :]
            return tile

        def pre_norm_dve(dve, gain):
            dve.wait_ge(S["rstd"], S.next("dve", "rstd"))
            for k in range(8):
                nc.vector.scalar_tensor_tensor(H[:, k, :], X[:, k, :], vcol(gain, k), R2, ALU.mult, ALU.mult
                                               ).then_inc(S["h_ready"], 1)

        def post_norm_dve(dve, name, gain):
            for k in range(8):
                bank, done = product_ready(dve, name, k)
                nc.vector.tensor_copy(H[:, k, :], bank).then_inc(done, 1)
            dve.wait_ge(S["rstd"], S.next("dve", "rstd"))
            for k in range(9):
                if k < 8:
                    nc.vector.scalar_tensor_tensor(H[:, k, :], H[:, k, :], vcol(gain, k), R2, ALU.mult, ALU.mult
                                                   ).then_inc(S["scaled"], 1)
                if k:
                    dve.wait_ge(S["scaled"], S.next("dve", "scaled"))
                    nc.vector.tensor_tensor(X[:, k - 1, :], X[:, k - 1, :], H[:, k - 1, :], ALU.add
                                            ).then_inc(S["x_new"], 1)

        def post_norm_act(act, name, sq):
            for k in range(8):
                drained(act, name, k)
                nc.scalar.activation(sq(k), H[:, k, :], ACT.Square).then_inc(S["squared"], 1)
            norm_power(act, PS[:, 5, :], R2, D)

        PROB = A[:, 24:28, :]
        PT_ = (A[:, 28:32, :], A[:, 32:36, :])
        AMX, ANM, ASUM, AREC = (small[:, 256 + 32 * j:288 + 32 * j] for j in range(4))

        def attention_tensor(pe, s, heads, parts, v_tok, rows):
            def score(h, qt):
                n = (qt + 1) * P
                both = parts(h)
                for j, (q, k) in enumerate(both):
                    mm = nc.tensor.matmul(PS[:, qt, 0:n], q[:, qt * P:n], k[:, 0:n], start=j == 0, stop=j == len(both) - 1)
                mm.then_inc(S[s + "scores"], 1)

            for qt in range(TT):
                score(0, qt)
            for h in range(heads):
                for qt in range(TT):
                    u = TT * h + qt
                    pe.wait_ge(S[s + "probs"], u + 1)
                    if u >= 2:
                        pe.wait_ge(S[s + "turned"], u - 1)
                    for kt in range(qt + 1):
                        mm = nc.tensor.transpose(PS[:, 4 + u % 2, kt * P:(kt + 1) * P], PROB[:, qt, kt * P:(kt + 1) * P], ident)
                    mm.then_inc(S[s + "turn"], 1)
                    if h + 1 < heads:
                        score(h + 1, qt)
                pe.wait_ge(S[s + "turned"], TT * h + TT)
                if h >= 2:
                    pe.wait_ge(S[s + "heads"], h - 1)
                o = PS[rows(h), 6 + h % 2, :]
                for kt in range(TT):
                    mm = nc.tensor.matmul(o[:, kt * P:], v_tok(h, kt), PT_[h % 2][:, kt, kt * P:], start=kt == 0, stop=True,
                                          skip_group_check=kt > 0)
                mm.then_inc(S[s + "out"], 1)

        def attention_act(act, s, heads, scale, dest, rows):
            units = TT * heads

            def turned(u):
                h, qt = u // TT, u % TT
                act.wait_ge(S[s + "turn"], u + 1)
                if h >= 2 and qt == 0:
                    act.wait_ge(S[s + "out"], h - 1)
                nc.scalar.activation(PT_[h % 2][:, 0:qt + 1, qt * P:(qt + 1) * P], as_tiles(PS[:, 4 + u % 2, 0:(qt + 1) * P]),
                                     ACT.Copy).then_inc(S[s + "turned"], 1)

            def leave(h):
                act.wait_ge(S[s + "out"], h + 1)
                nc.scalar.activation(dest(h), PS[rows(h), 6 + h % 2, :], ACT.Copy).then_inc(S[s + "heads"], 1)

            for u in range(units):
                n = (u % TT + 1) * P
                act.wait_ge(S[s + "max"], u + 1)
                nc.scalar.activation(PROB[:, u % TT, 0:n], PS[:, u % TT, 0:n], ACT.Exp, scale=scale, bias=ANM[:, u:u + 1],
                                     accum_out=ASUM[:, u:u + 1]).then_inc(S[s + "exp"], 1)
                if u:
                    turned(u - 1)
                if u % TT == 2 and u >= TT:
                    leave(u // TT - 1)
            turned(units - 1)
            leave(heads - 1)

        def attention_dve(dve, s, heads, scale):
            def normalise(u):
                dve.wait_ge(S[s + "exp"], u + 1)
                link(dve, "dve", nc.vector.reciprocal(AREC[:, u:u + 1], ASUM[:, u:u + 1]))
                n = (u % TT + 1) * P
                nc.vector.tensor_scalar(PROB[:, u % TT, 0:n], PROB[:, u % TT, 0:n], AREC[:, u:u + 1], None, ALU.mult
                                        ).then_inc(S[s + "probs"], 1)

            for u in range(TT * heads):
                qt = u % TT
                dve.wait_ge(S[s + "scores"], u + 1)
                own = PS[:, qt, qt * P:(qt + 1) * P]
                link(dve, "dve", nc.vector.tensor_tensor(own, own, ccol("future", 0, P), ALU.add))
                link(dve, "dve", nc.vector.tensor_reduce(AMX[:, u:u + 1], PS[:, qt, 0:(qt + 1) * P], AX.X, ALU.max))
                nc.vector.tensor_scalar(ANM[:, u:u + 1], AMX[:, u:u + 1], -scale, None, ALU.mult).then_inc(S[s + "max"], 1)
                if u:
                    normalise(u - 1)
            normalise(TT * heads - 1)

        half64 = lambda h: slice(64 * (h % 2), 64 * (h % 2) + 64)
        RT, KT2, VT2, LO, GD, MQ, MK, MV, MU, MG = 0, 3, 6, 9, 10, 11, 14, 17, 20, 22
        MVTOK = A[:, 36:39, :].rearrange("p a t -> p (a t)").rearrange("p (t c) -> p t c", t=TT)
        GVTOK = A[:, 39:41, :].rearrange("p a t -> p (a t)").rearrange("p (t c) -> p t c", t=TT)
        WS = a(41)
        GSQ = (a(42), a(43))
        MIX2 = [RT, RT + 1, RT + 2, MQ, MQ + 1, MQ + 2, MU, MU + 1]
        moba_parts = lambda h: [(A[half64(h), MQ + h // 2, :], A[half64(h), MK + h // 2, :])]

        def second_tensor(pe):
            pre_norm_tensor(pe)
            linear("win2", normed_input(pe))
            all_drained(pe, "win2", 24)
            for j in range(2):
                mm = nc.tensor.matmul(PS[:, 4, :], ones, a(MG + j), start=j == 0, stop=j == 1)
            mm.then_inc(S["g_mean"], 1)
            norm_sum(pe, lambda k: GSQ[k], 2, PS[:, 5, :])
            pe.wait_ge(S["g_norm"], 1)
            for j in range(2):
                for tt in range(TT):
                    mm = nc.tensor.transpose(PS[:, 6 + j, tt * P:(tt + 1) * P], a(MG + j)[:, tt * P:(tt + 1) * P], ident)
                mm.then_inc(S["g_turn"], 1)
            pe.wait_ge(S["g_turned"], 2)
            for g in range(4):
                for tt in range(TT):
                    mm = nc.tensor.matmul(PS[half64(g), 4 + g // 2, tt * P:(tt + 1) * P], GVTOK[:, tt, 64 * g:64 * g + 64],
                                          WS[:, g * P:(g + 1) * P], start=True, stop=True)
            mm.then_inc(S["g_mix"], 1)
            for j in range(3):
                for tt in range(TT):
                    mm = nc.tensor.transpose(PS[:, 1 + j, tt * P:(tt + 1) * P], a(MV + j)[:, tt * P:(tt + 1) * P], ident)
                mm.then_inc(S["m_v"], 1)
            pe.wait_ge(S["m_vtok"], 3)
            pe.wait_ge(S["g_out"], 2)
            attention_tensor(pe, "m_", HEADS2, moba_parts, lambda h, kt: MVTOK[:, kt, 64 * h:64 * h + 64], half64)
            rwkv_tensor(pe)
            pe.wait_ge(S["mixed2"], PAIRS2)
            products("wout2", range(8), 8, lambda k: a(MIX2[k]))
            norm_sum(pe, lambda k: a(24 + k), 8, PS[:, 5, :])
            pre_norm_tensor(pe)
            linear("ffin2", normed_input(pe))
            all_drained(pe, "ffin2", 2 * NFF2)
            products("ffout2", range(8), NFF2, lambda k: a(k))
            norm_sum(pe, lambda k: a(24 + k), 8, PS[:, 5, :])

        def second_act(act):
            pre_norm_act(act)
            for f in range(24):
                if f >= 20 or f % 2:
                    bank, done = product_ready(act, "win2", f)
                    nc.scalar.activation(a(f), bank, ACT.Gelu_apprx_tanh if f >= 20 else ACT.Copy).then_inc(done, 1)
            for j in range(2):
                act.wait_ge(S["g_centre"], j + 1)
                nc.scalar.activation(GSQ[j], a(MG + j), ACT.Square).then_inc(S["squared"], 1)
            norm_power(act, PS[:, 5, :], a(44), 2 * P)
            for j in range(2):
                act.wait_ge(S["g_turn"], j + 1)
                nc.scalar.activation(GVTOK[:, :, j * P:(j + 1) * P], as_tiles(PS[:, 6 + j, :]), ACT.Copy
                                     ).then_inc(S["g_turned"], 1)
            for j in range(3):
                act.wait_ge(S["m_v"], j + 1)
                nc.scalar.activation(MVTOK[:, :, j * P:(j + 1) * P], as_tiles(PS[:, 1 + j, :]), ACT.Copy
                                     ).then_inc(S["m_vtok"], 1)
            attention_act(act, "m_", HEADS2, 64 ** -0.5, lambda h: A[half64(h), MQ + h // 2, :], half64)
            rwkv_act(act)
            post_norm_act(act, "wout2", lambda k: a(24 + k))
            pre_norm_act(act)
            for j in range(NFF2):
                bank, done = product_ready(act, "ffin2", 2 * j)
                if j >= 2:
                    drained(act, "ffin2", 2 * j - 3)
                nc.scalar.activation(a(22 + j % 2), bank, ACT.Silu).then_inc(done, 1)
            post_norm_act(act, "ffout2", lambda k: a(24 + k))

        def second_dve(dve):
            pre_norm_dve(dve, "pre_mix")
            for f in range(0, 20, 2):
                bank, done = product_ready(dve, "win2", f)
                nc.vector.tensor_copy(a(f), bank).then_inc(done, 1)
            nc.vector.tensor_tensor(as_tiles(WS), as_tiles(vcol("ws", 0, 512)),
                                    ccol("le", 0, P).unsqueeze(1).to_broadcast([P, 4, P]), ALU.mult)
            all_drained(dve, "win2", 24)
            dve.wait_ge(S["g_mean"], 1)
            for j in range(2):
                nc.vector.scalar_tensor_tensor(a(MG + j), PS[:, 4, :], -1.0 / (2 * P), a(MG + j), ALU.mult, ALU.add
                                               ).then_inc(S["g_centre"], 1)
            dve.wait_ge(S["rstd"], S.next("dve", "rstd"))
            for j in range(2):
                link(dve, "dve", nc.vector.scalar_tensor_tensor(a(MG + j), a(MG + j), vcol("ln_g", j), a(44), ALU.mult, ALU.mult))
                v = nc.vector.tensor_scalar(a(MG + j), a(MG + j), vcol("ln_b", j), None, ALU.add)
            v.then_inc(S["g_norm"], 1)
            dve.wait_ge(S["g_mix"], 1)
            for j in range(2):
                link(dve, "dve", nc.vector.tensor_tensor(as_tiles(GSQ[j]), as_tiles(PS[:, 4 + j, :]),
                                                         vcol("bs", j * P, P).unsqueeze(1).to_broadcast([P, TT, P]), ALU.add))
                nc.vector.tensor_tensor(a(MU + j), a(MU + j), GSQ[j], ALU.mult).then_inc(S["g_out"], 1)
            attention_dve(dve, "m_", HEADS2, 64 ** -0.5)
            rwkv_dve(dve)
            post_norm_dve(dve, "wout2", "post_mix")
            pre_norm_dve(dve, "pre_ffn")
            for j in range(NFF2):
                bank, done = product_ready(dve, "ffin2", 2 * j + 1)
                drained(dve, "ffin2", 2 * j)
                nc.vector.tensor_tensor(a(j), a(22 + j % 2), bank, ALU.mult).then_inc(done, 1)
            post_norm_dve(dve, "ffout2", "post_ffn")

        def second_pool(pool):
            pool.wait_ge(S["x_new"], 8)
            pool.dma_start(LEVELS, levels_in).then_inc(S["levels"], 16)

        C = float(np.exp(-0.5))
        MID, END = P // 2 - 1, P - 1
        SW, LL, KK = (22, 23, 24), (25, 26, 27), (28, 29, 30)
        EX = ((37, 38, 39), (40, 41, 42), (43, 44, 45))
        BI, KX = (46, 47, 48), (KT2, KT2 + 1, KT2 + 2)
        KR = [A[:, 14 + 2 * p:16 + 2 * p, :].rearrange("p a t -> p (a t)").rearrange("p (c q t) -> p c q t", c=4, q=2)
              for p in range(3)]
        SC2 = [A[:, 22 + 4 * h:26 + 4 * h, :].rearrange("p c (q t) -> p c q t", q=4) for h in range(6)]
        tok384 = lambda v: v.rearrange("p a t -> p (a t)").rearrange("p (c i) -> p c i", c=4)
        TOK2 = (tok384(A[:, 49:52, :]), tok384(H[:, 0:3, :]), tok384(H[:, 3:6, :]))
        YI = (H[:, 6, :], H[:, 7, :], a(52))
        WU = (a(46)[:, 0:384], a(47)[:, 0:384])
        STATE = a(48)[:, 0:192].rearrange("p (a i) -> p a i", a=3)
        LM = small[:, 384:396].rearrange("p (a c) -> p a c", a=3)
        LE = small[:, 396:408].rearrange("p (a c) -> p a c", a=3)
        SCL = small[:, 408:420].rearrange("p (a c) -> p a c", a=3)

        def rwkv_tensor(pe):
            pe.wait_ge(S["lora_in"], 2)
            for f in range(6):
                bank = open_bank("lora2", f)
                rows = slice(0, 64) if f < 3 else slice(64, 128)
                nc.tensor.matmul(bank, vec[rows, VOFF["w2a2"][0] + f % 3 * P:VOFF["w2a2"][0] + (f % 3 + 1) * P],
                                 A[rows, LO, :], start=True, stop=True).then_inc(S["product"], 1)
            for p in range(3):
                pe.wait_ge(S["squared"], S.next("pe", "squared"))
                nc.tensor.matmul(PS[:, 4 + p, :], ones64, a(31 + p), start=True, stop=True).then_inc(S["kk_sum"], 1)
            n = 0
            for p in range(3):
                pe.wait_ge(S["prep"], p + 1)
                for src in (VT2 + p, BI[p], KX[p]):
                    if n == 0:
                        pe.wait_ge(S["kk_max"], 3)
                    if n >= 2:
                        pe.wait_ge(S["tok"], n - 1)
                    for c in range(4):
                        mm = nc.tensor.transpose(PS[:, 4 + n % 2, c * P:(c + 1) * P], a(src)[:, c * P:(c + 1) * P], ident)
                    mm.then_inc(S["tok_turn"], 1)
                    n += 1
            all_drained(pe, "lora2", 6)
            for h in range(6):
                rows, p = half64(h), h // 2
                for c in range(4):
                    m = 4 * h + c
                    if m >= 4:
                        pe.wait_ge(S["within_out"], m - 3)
                    s = slice(c * P, (c + 1) * P)
                    rhs = KR[p][rows, c, :, :].rearrange("p q t -> p (q t)")
                    nc.tensor.matmul(PS[:, m % 4, 0:256], a(BI[p])[rows, s], rhs, start=True, stop=True)
                    nc.tensor.matmul(PS[:, m % 4, 256:512], a(KX[p])[rows, s], rhs, start=True, stop=True
                                     ).then_inc(S["within"], 1)
            pe.wait_ge(S["tok"], 9)
            pe.wait_ge(S["within_out"], 24)
            q = 0
            for g in range(2):
                for n in range(INV_LEVELS):
                    for j in range(3):
                        h, s = 3 * g + j, (g * INV_LEVELS + n) * 3 + j
                        pe.wait_ge(S["inv_start"], g + 1)
                        if n:
                            pe.wait_ge(S["inv_used"], 2 * (s - 3) + 2)
                        for c in range(4):
                            mm = nc.tensor.matmul(PS[:, j, c * P:(c + 1) * P], SC2[h][:, c, 0, :],
                                                  a(BI[j])[:, c * P:(c + 1) * P], start=True, stop=True)
                        mm.then_inc(S["nx"], 1)
                    for j in range(3):
                        s = (g * INV_LEVELS + n) * 3 + j
                        pe.wait_ge(S["nx_out"], s + 1)
                        for turned in range(2):
                            if q >= 5:
                                pe.wait_ge(S["inv_used"], q - 4)
                            for c in range(4):
                                t = slice(c * P, (c + 1) * P)
                                l, r = (YI[j][:, t], a(KX[j])[:, t]) if turned else (a(KX[j])[:, t], YI[j][:, t])
                                mm = nc.tensor.matmul(PS[:, 3 + q % 5, t], l, r, start=True, stop=True)
                            mm.then_inc(S["xnx"], 1)
                            q += 1
            pe.wait_ge(S["inv_kept"], 6)
            for c in range(4):
                if c:
                    pe.wait_ge(S["state"], c)
                for h in range(6):
                    rows, p, i = half64(h), h // 2, slice(64 * h, 64 * h + 64)
                    o = PS[:, (0, 5)[h % 2], p * 64:p * 64 + 64]
                    if c:
                        nc.tensor.matmul(o, KR[p][rows, c, 0, :], STATE[rows, p, :], start=True, stop=False)
                    mm = nc.tensor.matmul(o, SC2[h][:, c, 2, :], TOK2[0][:, c, i], start=c == 0, stop=True)
                mm.then_inc(S["w"], 1)
                pe.wait_ge(S["w_out"], c + 1)
                for h in range(6):
                    i = slice(64 * h, 64 * h + 64)
                    mm = nc.tensor.matmul(PS[:, 1, i], SC2[h][:, c, 0, :], WU[0][:, i], start=True, stop=True)
                mm.then_inc(S["u"], 1)
                pe.wait_ge(S["u_out"], c + 1)
                for h in range(6):
                    rows, p, i = half64(h), h // 2, slice(64 * h, 64 * h + 64)
                    o = PS[rows, 4, p * 64:p * 64 + 64]
                    nc.tensor.matmul(o, TOK2[1][:, c, i], WU[1][:, i], start=True, stop=False)
                    mm = nc.tensor.matmul(o, TOK2[2][:, c, i], TOK2[0][:, c, i], start=False, stop=True)
                mm.then_inc(S["delta"], 1)
                if c:
                    pe.wait_ge(S["y_kept"], c)
                for h in range(6):
                    rows, p, i = half64(h), h // 2, slice(64 * h, 64 * h + 64)
                    o = PS[rows, 2, p * P:(p + 1) * P]
                    if c:
                        nc.tensor.matmul(o, STATE[rows, p, :], KR[p][rows, c, 1, :], start=True, stop=False)
                    nc.tensor.matmul(o, WU[1][:, i], SC2[h][:, c, 1, :], start=c == 0, stop=False)
                    mm = nc.tensor.matmul(o, TOK2[0][:, c, i], SC2[h][:, c, 3, :], start=False, stop=True)
                mm.then_inc(S["y_chunk"], 1)
            pe.wait_ge(S["y_kept"], 4)
            for p in range(3):
                nc.tensor.matmul(PS[:, 4 + p, :], ones64, a(KX[p]), start=True, stop=True).then_inc(S["y_mean"], 1)
            pe.wait_ge(S["y_centre"], 3)
            for p in range(3):
                pe.wait_ge(S["squared"], S.next("pe", "squared"))
                nc.tensor.matmul(PS[:, 4 + p, :], ones64, a(31 + p), start=True, stop=True).then_inc(S["summed"], 1)
            for p in range(3):
                nc.tensor.matmul(PS[:, (0, 1, 7)[p], :], ones64, a(RT + p), start=True, stop=True).then_inc(S["bonus"], 1)
            pe.wait_ge(S["bonus_out"], 3)
            for p in range(3):
                g = (BANK0["gate2"] + p) % 4
                bank = open_bank("gate2", p)
                nc.tensor.matmul(bank, vcol("g2", p * P, P), a(GD), start=True, stop=True).then_inc(S["product"], 1)

        def rwkv_act(act):
            act.wait_ge(S["shifted"], 1)
            nc.scalar.activation(A[0:64, LO, :], A[0:64, LO, :], ACT.Tanh).then_inc(S["lora_in"], 1)
            nc.scalar.activation(a(GD), a(GD), ACT.Sigmoid).then_inc(S["lora_in"], 1)
            for f in range(6):
                bank, done = product_ready(act, "lora2", f)
                dst, b = (SW[f], "w0") if f < 3 else (BI[f - 3], "a0")
                nc.scalar.activation(a(dst), bank, ACT.Sigmoid, bias=vcol(b, f % 3)).then_inc(done, 1)
            for p in range(3):
                act.wait_ge(S["kk_raw"], p + 1)
                nc.scalar.activation(a(31 + p), a(KK[p]), ACT.Square).then_inc(S["squared"], 1)
            for p in range(3):
                act.wait_ge(S["kk_max"], p + 1)
                link(act, "act", nc.scalar.activation(a(34 + p), a(34 + p), ACT.Ln, scale=2.0 ** 20))
                nc.scalar.activation(a(34 + p), a(34 + p), ACT.Exp, scale=-0.5, bias=ccol("eps", 2)).then_inc(S["kk_inv"], 1)
            for p in range(3):
                act.wait_ge(S["logs"], p + 1)
                nc.scalar.activation(a(EX[p][0]), a(LL[p]), ACT.Exp, scale=-C)
                nc.scalar.activation(a(EX[p][1]), a(LL[p]), ACT.Exp, scale=C)
                nc.scalar.activation(a(EX[p][2]), a(SW[p]), ACT.Exp, scale=-C).then_inc(S["decays"], 1)
            act.wait_ge(S["scl_in"], 1)
            nc.scalar.activation(SCL, SCL, ACT.Exp, scale=-C).then_inc(S["scl"], 1)
            for n in range(9):
                act.wait_ge(S["tok_turn"], n + 1)
                p = n // 3
                nc.scalar.activation(TOK2[n % 3][:, :, p * P:(p + 1) * P], as_tiles(PS[:, 4 + n % 2, :]), ACT.Copy
                                     ).then_inc(S["tok"], 1)
            for s in range(2 * INV_LEVELS * 3):
                act.wait_ge(S["nx"], s + 1)
                nc.scalar.activation(YI[s % 3], PS[:, s % 3, :], ACT.Copy).then_inc(S["nx_out"], 1)
            for c in range(4):
                act.wait_ge(S["w"], c + 1)
                for b, bank in enumerate((0, 5)):
                    v = nc.scalar.activation(WU[0].rearrange("p (a b i) -> p a b i", b=2, i=64)[:, :, b, :],
                                             PS[:, bank, 0:192].rearrange("p (a i) -> p a i", i=64), ACT.Copy)
                v.then_inc(S["w_out"], 1)
                act.wait_ge(S["y_chunk"], c + 1)
                nc.scalar.activation(A[:, KT2:KT2 + 3, c * P:(c + 1) * P], as_tiles(PS[:, 2, 0:384]), ACT.Copy
                                     ).then_inc(S["y_kept"], 1)
            for p in range(3):
                act.wait_ge(S["y_centre"], p + 1)
                nc.scalar.activation(a(31 + p), a(KX[p]), ACT.Square).then_inc(S["squared"], 1)
            for p in range(3):
                norm_power(act, PS[:, 4 + p, :], a(34 + p), 64, eps_col=ccol("eps", 1))

        def rwkv_dve(dve):
            tmp = (a(22), a(23))
            for j in range(11):
                cur, t = a(j), tmp[j % 2]
                nc.vector.tensor_tensor(t[:, 1:], cur[:, :-1], cur[:, 1:], ALU.subtract)
                link(dve, "dve", nc.vector.tensor_scalar(t[:, 0:1], cur[:, 0:1], -1.0, None, ALU.mult))
                v = nc.vector.scalar_tensor_tensor(cur, t, vcol("mu", j), cur, ALU.mult, ALU.add)
            v.then_inc(S["shifted"], 1)
            dve.wait_ge(S["shifted"], 1)
            for p in range(3):
                nc.vector.tensor_scalar(a(KK[p]), a(KT2 + p), vcol("k_k", p), None, ALU.mult).then_inc(S["kk_raw"], 1)
            for p in range(3):
                dve.wait_ge(S["kk_sum"], p + 1)
                nc.vector.tensor_scalar(a(34 + p), PS[:, 4 + p, :], 1e-24, None, ALU.max).then_inc(S["kk_max"], 1)
            all_drained(dve, "lora2", 6)
            by_chunk = lambda t: t.rearrange("p (c t) -> p c t", c=4)
            for p in range(3):
                l = by_chunk(a(LL[p]))
                for c in range(4):
                    v = nc.vector.tensor_tensor_scan(l[:, c, :], ones, by_chunk(a(SW[p]))[:, c, :], 0.0, ALU.mult, ALU.add)
                link(dve, "dve", v)
                nc.vector.tensor_copy(LE[:, p, :].unsqueeze(2), l[:, :, END:END + 1])
                link(dve, "dve", nc.vector.tensor_copy(LM[:, p, :].unsqueeze(2), l[:, :, MID:MID + 1]))
                link(dve, "dve", nc.vector.tensor_tensor(l, l, LM[:, p, :].unsqueeze(2).to_broadcast([P, 4, P]), ALU.subtract))
                nc.vector.tensor_tensor(a(SW[p]), a(LL[p]), a(SW[p]), ALU.subtract).then_inc(S["logs"], 1)
            link(dve, "dve", nc.vector.tensor_tensor(SCL, LE, LM, ALU.subtract))
            nc.vector.tensor_tensor(SCL[:, :, 0:3], SCL[:, :, 0:3], LM[:, :, 1:4], ALU.add).then_inc(S["scl_in"], 1)
            for p in range(3):
                e_r, e_k, e_p = (a(t) for t in EX[p])
                k, kk, b, r = a(KT2 + p), a(KK[p]), a(BI[p]), a(RT + p)
                dve.wait_ge(S["kk_inv"], p + 1)
                link(dve, "dve", nc.vector.tensor_tensor(kk, kk, a(34 + p), ALU.mult))
                link(dve, "dve", nc.vector.tensor_scalar(a(31), b, 1.0, vcol("k_a", p), ALU.subtract, ALU.mult))
                link(dve, "dve", nc.vector.scalar_tensor_tensor(k, a(31), 1.0, k, ALU.add, ALU.mult))
                link(dve, "dve", nc.vector.scalar_tensor_tensor(b, kk, -1.0, b, ALU.mult, ALU.mult))
                dve.wait_ge(S["decays"], p + 1)
                nc.vector.tensor_tensor(b, b, e_k, ALU.mult)
                nc.vector.tensor_tensor(KR[p][:, :, 0, :], by_chunk(kk), by_chunk(e_p), ALU.mult)
                link(dve, "dve", nc.vector.tensor_tensor(KR[p][:, :, 1, :], by_chunk(r), by_chunk(e_r), ALU.mult))
                link(dve, "dve", nc.vector.scalar_tensor_tensor(r, r, vcol("r_k", p), k, ALU.mult, ALU.mult))
                nc.vector.tensor_tensor(k, k, e_k, ALU.mult).then_inc(S["prep"], 1)
            for m in range(24):
                dve.wait_ge(S["within"], m + 1)
                src = PS[:, m % 4, :].rearrange("p (q t) -> p q t", q=4)
                dst = SC2[m // 4][:, m % 4, :, :]
                for q, mask in ((0, "lt"), (1, "le")):
                    v = nc.vector.tensor_tensor(dst[:, q::2, :], src[:, q::2, :],
                                                ccol(mask, 0, P).unsqueeze(1).to_broadcast([P, 2, P]), ALU.mult)
                v.then_inc(S["within_out"], 1)
            dve.wait_ge(S["tok"], 9)
            dve.wait_ge(S["levels"], 16)
            q = 0
            for g in range(2):
                wide_ident = ident.unsqueeze(1).to_broadcast([P, 4, P])
                if g:
                    dve.wait_ge(S["inv_kept"], 3)
                for j in range(3):
                    nc.vector.tensor_copy(as_tiles(a(BI[j])), wide_ident)
                    v = nc.vector.tensor_copy(as_tiles(a(KX[j])), wide_ident)
                v.then_inc(S["inv_start"], 1)
                dve.wait_ge(S["inv_start"], g + 1)
                for n in range(INV_LEVELS):
                    for j in range(3):
                        for turned, dst in enumerate((BI[j], KX[j])):
                            dve.wait_ge(S["xnx"], q + 1)
                            if not turned:
                                dve.wait_ge(S["xnx"], q + 2)
                            mask = level(n, turned).bitcast(U32).unsqueeze(1).to_broadcast([P, 4, P])
                            nc.vector.copy_predicated(as_tiles(a(dst)), mask, as_tiles(PS[:, 3 + q % 5, :])
                                                      ).then_inc(S["inv_used"], 1)
                            q += 1
                dve.wait_ge(S["inv_used"], q)
                for j in range(3):
                    nc.vector.tensor_copy(SC2[3 * g + j][:, :, 0, :], as_tiles(a(KX[j]))).then_inc(S["inv_kept"], 1)
            for c in range(4):
                dve.wait_ge(S["u"], c + 1)
                nc.vector.tensor_copy(WU[1], PS[:, 1, 0:384]).then_inc(S["u_out"], 1)
                dve.wait_ge(S["delta"], c + 1)
                if c < 3:
                    d = PS[:, 4, 0:192].rearrange("p (a i) -> p a i", a=3)
                    dve.wait_ge(S["y_chunk"], c + 1)
                    dve.wait_ge(S["scl"], 1)
                    if c:
                        link(dve, "dve", nc.vector.tensor_tensor(STATE, STATE, d, ALU.add))
                    else:
                        link(dve, "dve", nc.vector.tensor_copy(STATE, d))
                    nc.vector.tensor_tensor(STATE, STATE, SCL[:, :, c:c + 1].to_broadcast([P, 3, 64]), ALU.mult
                                            ).then_inc(S["state"], 1)
            dve.wait_ge(S["y_kept"], 4)
            for p in range(3):
                dve.wait_ge(S["y_mean"], p + 1)
                nc.vector.scalar_tensor_tensor(a(KX[p]), PS[:, 4 + p, :], -1.0 / 64, a(KX[p]), ALU.mult, ALU.add
                                               ).then_inc(S["y_centre"], 1)
            for p in range(3):
                dve.wait_ge(S["bonus"], p + 1)
                nc.vector.tensor_tensor(a(37 + p), PS[:, (0, 1, 7)[p], :], a(VT2 + p), ALU.mult).then_inc(S["bonus_out"], 1)
            dve.wait_ge(S["bonus_out"], 3)
            for p in range(3):
                y = a(KX[p])
                dve.wait_ge(S["rstd"], S.next("dve", "rstd"))
                link(dve, "dve", nc.vector.scalar_tensor_tensor(y, y, vcol("lnx_g", p), a(34 + p), ALU.mult, ALU.mult))
                link(dve, "dve", nc.vector.scalar_tensor_tensor(y, y, vcol("lnx_b", p), a(37 + p), ALU.add, ALU.add))
            for p in range(3):
                bank, done = product_ready(dve, "gate2", p)
                nc.vector.tensor_tensor(a(RT + p), a(KX[p]), bank, ALU.mult).then_inc(done, 1)
            for p in range(3):
                drained(dve, "gate2", p)
            dve.sem_inc(S["mixed2"], 3)

        CQ, CKV, KROPE, GLU_A, GLU_B = 0, 3, 5, 6, 14
        QN, QR, COS, SIN, ANG, NUM = 8, 16, 20, 21, 22, 23
        KN, YA, GA3, GC3 = 36, 36, 22, 44
        VTOK3 = A[:, 44:52, :].rearrange("p (a b) t -> p a (b t)", a=TT)
        TWO_PI = (6.28125, 8117 / 2.0 ** 22, float(2 * np.pi - 6.28125 - 8117 / 2.0 ** 22))
        ROUND = 1.5 * 2.0 ** 23
        full = lambda h: slice(0, P)
        mla_parts = lambda h: [(a(QN + h), a(KN + h)),
                               (A[half64(h), QR + h // 2, :], A[half64(h), KROPE, :])]

        def third_tensor(pe):
            pre_norm_tensor(pe)
            products("win3a", range(8), 8, normed_input(pe))
            norm_sum(pe, lambda k: a(24 + k), 3, PS[:, 5, :])
            norm_sum(pe, lambda k: a(27 + k), 2, PS[:, 6, :])
            pe.wait_ge(S["low_rank"], 1)
            products("uqkv3", range(12), 3, lambda k: a(CQ + k))
            products("uqkv3", range(12, 20), 2, lambda k: a(CKV + k), tile0=36)
            for f in range(20, 28):
                half, tt = (f - 20) // TT, (f - 20) % TT
                bank = open_bank("uqkv3", f)
                for k in range(2):
                    n = 52 + 4 * (2 * half + k)
                    mm = nc.tensor.matmul(bank, a(CKV + k)[:, tt * P:(tt + 1) * P], weight_tile("uqkv3", n, 4),
                                          start=k == 0, stop=k == 1)
                mm.then_inc(S["product"], 1)
            all_drained(pe, "uqkv3", 28)
            for j in range(5):
                src = KROPE if j == 4 else QR + j
                mm = nc.tensor.matmul(PS[:, (4, 5, 6, 7, 0)[j], :], ccol("swap", 0, P), a(src), start=True, stop=True)
                if j == 0:
                    mm.then_inc(S["chunk_used"], 1)
                else:
                    mm.then_inc(S["swapped"], 1)
            pe.wait_ge(S["roped"], 5)
            attention_tensor(pe, "l_", HEADS3, mla_parts, lambda h, kt: VTOK3[:, kt, h * P:(h + 1) * P], full)
            pe.wait_ge(S["l_heads"], HEADS3)
            products("wo3", range(8), 8, lambda k: a(QN + k))
            products("win3b", range(30), 8, lambda k: H[:, k, :])
            for k in range(8):
                pe.wait_ge(S["conv"], k + 1)
                mm = nc.tensor.matmul(PS[:, 4, :], ones, a(GLU_B + k), start=k == 0, stop=k == 7)
            mm.then_inc(S["conv_mean"], 1)
            norm_sum(pe, lambda k: a(GLU_A + k), 8, PS[:, 5, :])
            pe.wait_ge(S["conv_act"], 8)
            products("pw3", range(8), 8, lambda k: a(GLU_B + k))
            pe.wait_ge(S["merged"], 8)
            products("wout3", range(8), 8, lambda k: a(GC3 + k))
            norm_sum(pe, lambda k: a(24 + k), 8, PS[:, 5, :])
            pre_norm_tensor(pe)
            linear("ff1_3", normed_input(pe))
            pe.wait_ge(S["hidden3"], NFF3)
            products("ff2_3", range(8), NFF3, lambda k: a(k))
            norm_sum(pe, lambda k: a(32 + k), 8, PS[:, 5, :])

        def third_act(act):
            pre_norm_act(act)
            for f in range(8):
                bank, done = product_ready(act, "win3a", f)
                nc.scalar.activation(a(f), bank, ACT.Copy).then_inc(done, 1)
            for f in range(5):
                drained(act, "win3a", f)
                nc.scalar.activation(a(24 + f), a(f), ACT.Square).then_inc(S["squared"], 1)
            norm_power(act, PS[:, 5, :], a(30), 3 * P)
            norm_power(act, PS[:, 6, :], a(31), 2 * P)
            act.wait_ge(S["angles"], 2)
            nc.scalar.activation(a(COS), a(COS), ACT.Sin)
            nc.scalar.activation(a(SIN), a(SIN), ACT.Sin).then_inc(S["rotary"], 1)
            for f in range(0, 28):
                if f % 2 == 0:
                    bank, done = product_ready(act, "uqkv3", f)
                    nc.scalar.activation(third_uqkv(f), bank, ACT.Copy).then_inc(done, 1)
            attention_act(act, "l_", HEADS3, 192 ** -0.5, lambda h: a(QN + h), full)
            for k in range(8):
                bank, done = product_ready(act, "wo3", k)
                nc.scalar.activation(a(YA + k), bank, ACT.Copy).then_inc(done, 1)
            for f in range(30):
                bank, done = product_ready(act, "win3b", f)
                dst = a(8 + f) if f < 14 else a(GA3 + f - 14) if f < 22 else a(GC3 + f - 22)
                nc.scalar.activation(dst, bank, ACT.Copy if f < 6 else ACT.Sigmoid).then_inc(done, 1)
            for k in range(8):
                act.wait_ge(S["conv_centre"], k + 1)
                nc.scalar.activation(a(GLU_A + k), a(GLU_B + k), ACT.Square).then_inc(S["squared"], 1)
            norm_power(act, PS[:, 5, :], R2, D)
            for k in range(8):
                act.wait_ge(S["conv_norm"], k + 1)
                nc.scalar.activation(a(GLU_B + k), a(GLU_B + k), ACT.Silu, bias=vcol("ln3_b", k)).then_inc(S["conv_act"], 1)
            post_norm_act(act, "wout3", lambda k: a(24 + k))
            pre_norm_act(act)
            for f in range(NFF3):
                bank, done = product_ready(act, "ff1_3", f)
                nc.scalar.activation(a(f), bank, ACT.Relu).then_inc(done, 1)
            post_norm_act(act, "ff2_3", lambda k: a(32 + k))

        def third_uqkv(f):
            if f < 20:
                return a(QN + f if f < 8 else QR + f - 8 if f < 12 else KN + f - 12)
            half, tt = (f - 20) // TT, (f - 20) % TT
            return VTOK3[:, tt, half * T:(half + 1) * T]

        def third_dve(dve):
            pre_norm_dve(dve, "mix_pre3")
            dve.wait_ge(S["positions"], 16)
            link(dve, "dve", nc.vector.tensor_copy(a(ANG), a(COS).bitcast(I32)))
            link(dve, "dve", nc.vector.tensor_scalar(a(ANG), a(ANG), ccol("invf", 0), None, ALU.mult))
            for dst, shift in ((SIN, 0.0), (COS, 0.25)):
                link(dve, "dve", nc.vector.tensor_scalar(a(NUM), a(ANG), 1 / (2 * np.pi), shift, ALU.mult, ALU.add))
                link(dve, "dve", nc.vector.tensor_scalar(a(NUM), a(NUM), ROUND, ROUND, ALU.add, ALU.subtract))
                link(dve, "dve", nc.vector.scalar_tensor_tensor(a(dst), a(NUM), -TWO_PI[0], a(ANG), ALU.mult, ALU.add))
                for part in TWO_PI[1:]:
                    link(dve, "dve", nc.vector.scalar_tensor_tensor(a(dst), a(NUM), -part, a(dst), ALU.mult, ALU.add))
                link(dve, "dve", nc.vector.tensor_scalar(a(dst), a(dst), 2 * np.pi * shift, 3.1415925, ALU.add, ALU.min))
                nc.vector.tensor_scalar(a(dst), a(dst), -3.1415925, None, ALU.max).then_inc(S["angles"], 1)
            dve.wait_ge(S["rotary"], 1)
            link(dve, "dve", nc.vector.tensor_scalar(a(SIN), a(SIN), ccol("sgn", 0), None, ALU.mult))
            for base, n, r, gain in ((CQ, 3, 30, "q_norm"), (CKV, 2, 31, "kv_norm")):
                dve.wait_ge(S["rstd"], S.next("dve", "rstd"))
                for k in range(n):
                    v = nc.vector.scalar_tensor_tensor(a(base + k), a(base + k), vcol(gain, k), a(r), ALU.mult, ALU.mult)
            v.then_inc(S["low_rank"], 1)
            for f in range(28):
                if f % 2:
                    bank, done = product_ready(dve, "uqkv3", f)
                    nc.vector.tensor_copy(third_uqkv(f), bank).then_inc(done, 1)
            for j in range(5):
                t = a(KROPE if j == 4 else QR + j)
                dve.wait_ge(S["swapped"], max(j, 1))
                link(dve, "dve", nc.vector.tensor_tensor(a(NUM), PS[:, (4, 5, 6, 7, 0)[j], :], a(SIN), ALU.mult))
                link(dve, "dve", nc.vector.tensor_tensor(t, t, a(COS), ALU.mult))
                nc.vector.tensor_tensor(t, t, a(NUM), ALU.add).then_inc(S["roped"], 1)
                dve.wait_ge(S["roped"], j + 1)
            attention_dve(dve, "l_", HEADS3, 192 ** -0.5)
            for k0 in range(0, 8, 2):
                for k in (k0, k0 + 1):
                    drained(dve, "win3b", 6 + k)
                    link(dve, "dve", nc.vector.tensor_tensor(a(GLU_A + k), a(GLU_A + k), a(GLU_B + k), ALU.mult))
                for tap in reversed(range(TAPS3)):
                    s = TAPS3 - 1 - tap
                    for k in (k0, k0 + 1):
                        u, y, w = a(GLU_A + k), a(GLU_B + k), vcol("conv3", k * TAPS3 + tap)
                        if s == 0:
                            v = nc.vector.tensor_scalar(y, u, w, vcol("conv_b", k), ALU.mult, ALU.add)
                        else:
                            n = k0 // 2 * 2 * (TAPS3 - 1) + 2 * s + (k - k0) - 1
                            dve.wait_ge(S["tap"], n)
                            v = nc.vector.scalar_tensor_tensor(y[:, s:], u[:, :T - s], w, y[:, s:], ALU.mult, ALU.add)
                        if s < TAPS3 - 1:
                            v.then_inc(S["tap"], 1)
                        else:
                            v.then_inc(S["conv"], 1)
            dve.wait_ge(S["conv_mean"], 1)
            for k in range(8):
                nc.vector.scalar_tensor_tensor(a(GLU_B + k), PS[:, 4, :], -1.0 / D, a(GLU_B + k), ALU.mult, ALU.add
                                               ).then_inc(S["conv_centre"], 1)
            all_drained(dve, "win3b", 30)
            for k in range(8):
                v = nc.vector.tensor_tensor(a(GA3 + k), a(GA3 + k), a(YA + k), ALU.mult)
            link(dve, "dve", v)
            dve.wait_ge(S["rstd"], S.next("dve", "rstd"))
            for k in range(8):
                nc.vector.scalar_tensor_tensor(a(GLU_B + k), a(GLU_B + k), vcol("ln3_g", k), R2, ALU.mult, ALU.mult
                                               ).then_inc(S["conv_norm"], 1)
            for k in range(8):
                bank, done = product_ready(dve, "pw3", k)
                nc.vector.scalar_tensor_tensor(a(GC3 + k), bank, vcol("b_pw2", k), a(GC3 + k), ALU.add, ALU.mult
                                               ).then_inc(done, 1)
                drained(dve, "pw3", k)
                nc.vector.tensor_tensor(a(GC3 + k), a(GC3 + k), a(GA3 + k), ALU.add).then_inc(S["merged"], 1)
            post_norm_dve(dve, "wout3", "mix_post3")
            pre_norm_dve(dve, "mlp_pre3")
            for f in range(NFF3):
                drained(dve, "ff1_3", f)
                nc.vector.tensor_tensor(a(f), a(f), a(f), ALU.mult).then_inc(S["hidden3"], 1)
            post_norm_dve(dve, "ff2_3", "mlp_post3")

        def third_pool(pool):
            pool.wait_ge(S["x_new"], 24)
            pool.dma_start(a(COS).bitcast(I32), pos_in.partition_broadcast(P)).then_inc(S["positions"], 16)

        block = stack.enter_context(nc.Block())

        @block.sync
        def _(sp):
            first_sync(sp)
            sp.wait_ge(S["x_new"], 40)
            sp.dma_start(out, X[:, :, :]).then_inc(S["stored"], 16)
            sp.wait_ge(S["stored"], 16)

        @block.tensor
        def _(pe):
            first_tensor(pe)
            second_tensor(pe)
            third_tensor(pe)

        @block.scalar
        def _(act):
            first_act(act)
            second_act(act)
            third_act(act)

        @block.vector
        def _(dve):
            first_dve(dve)
            second_dve(dve)
            third_dve(dve)

        @block.gpsimd
        def _(pool):
            first_pool(pool)
            second_pool(pool)
            third_pool(pool)


def columns(v):
    return np.ascontiguousarray(v.reshape(-1, P).T)


def tiles_fk(w):
    k, f = w.shape
    return w.reshape(k // P, P, f // P, P).transpose(1, 2, 0, 3).reshape(P, -1)


def chunks(*laid):
    a = np.concatenate(laid, axis=1) if len(laid) > 1 else laid[0]
    n = -(-a.shape[1] // (WT * P))
    if a.shape[1] < n * WT * P:
        a = np.concatenate([a, np.zeros((P, n * WT * P - a.shape[1]), a.dtype)], axis=1)
    return a.reshape(P, n, WT * P).transpose(1, 0, 2)


def weight_stream(i):
    w_in = i["w_in"][0].reshape(D, -1, P)[:, ORDER1].reshape(D, -1)
    ada = i["w_ada"][0].reshape(KD, P, 12, T).transpose(2, 1, 0, 3).reshape(12, P, WT * P)
    out = [ada, chunks(tiles_fk(w_in)), chunks(tiles_fk(i["w_out"][0]))]
    for e in range(EXPERTS):
        wide = lambda w: w.reshape(2, 4, P, DFF1 // T, T).transpose(3, 0, 2, 1, 4)
        gate_up = np.stack([wide(i["w_gate"][0, e]), wide(i["w_up"][0, e])], axis=4)
        down = i["w_down"][0, e].reshape(4, 4, P, D).transpose(0, 2, 1, 3).reshape(4, P, WT * P)
        out += [gate_up.reshape(8, P, WT * P), down]
    f = i["w_ffn_in_2"][0]
    half = f.shape[1] // 2
    pairs = np.stack([f[:, :half].reshape(D, NFF2, P), f[:, half:].reshape(D, NFF2, P)], axis=2).reshape(D, -1)
    out += [chunks(tiles_fk(i["w_in_2"][0])), chunks(tiles_fk(i["w_out_2"][0])), chunks(tiles_fk(pairs)),
            chunks(tiles_fk(i["w_ffn_out_2"][0]))]
    w3 = i["w_in_3"][0]
    rope = np.concatenate([w3[:, 640:704], w3[:, 640:704]], axis=1)
    out += [chunks(tiles_fk(np.concatenate([w3[:, :640], rope, w3[:, 704:960]], axis=1)))]
    uq = i["w_uq_3"][0].reshape(-1, HEADS3, 192)
    uq = np.concatenate([uq[:, :, :P].reshape(-1, D), uq[:, :, P:].reshape(-1, D // 2)], axis=1)
    uv = i["w_uv_3"][0].reshape(2, P, 2, T).transpose(1, 2, 0, 3).reshape(P, -1)
    out += [chunks(tiles_fk(uq), tiles_fk(i["w_uk_3"][0].reshape(2 * P, D)), uv)]
    out += [chunks(tiles_fk(w)) for w in (i["w_o_attn_3"][0], w3[:, 960:], i["w_pw2_3"][0], i["w_out_3"][0],
                                          i["w_ff1_3"][0], i["w_ff2_3"][0])]
    return np.concatenate(out, axis=0)


def vectors(i):
    col = {
        "c2": np.stack([columns(i["c"][0]), columns(i["c_ctx"])], axis=2).reshape(P, 16),
        "b_ada": columns(i["b_ada"][0]), "norm_mix": columns(i["norm_mix"][0]),
        "norm_ffn": columns(i["norm_ffn"][0]), "norm_final": columns(i["norm_final"]),
        "lb": columns(i["lb_logits"]), "hg_norm": columns(i["hg_norm"][0]), "conv1": columns(i["conv_w"][0]),
        "w_router": i["w_router"][0].reshape(KD, P, EXPERTS).transpose(1, 0, 2).reshape(P, -1),
        "pre_mix": columns(i["pre_mix_g_2"][0]), "mu": columns(i["rwkv_mu_2"][0]), "w0": columns(i["rwkv_w0_2"][0]),
        "a0": columns(i["rwkv_a0_2"][0]), "k_k": columns(i["rwkv_k_k_2"][0]), "k_a": columns(i["rwkv_k_a_2"][0]),
        "r_k": columns(i["rwkv_r_k_2"][0]), "lnx_g": columns(i["rwkv_lnx_g_2"][0]),
        "lnx_b": columns(i["rwkv_lnx_b_2"][0]), "ln_g": columns(i["gmlp_ln_g_2"][0]),
        "ln_b": columns(i["gmlp_ln_b_2"][0]), "post_mix": columns(i["post_mix_g_2"][0]),
        "pre_ffn": columns(i["pre_ffn_g_2"][0]), "post_ffn": columns(i["post_ffn_g_2"][0]),
        "w2a2": np.concatenate([i["rwkv_w2_2"][0], i["rwkv_a2_2"][0]], axis=0), "g2": i["rwkv_g2_2"][0],
        "ws": i["gmlp_w_s_2"][0].transpose(2, 0, 1).reshape(P, -1),
        "bs": np.repeat(i["gmlp_b_s_2"][0].reshape(2, 2, 1, P), 64, axis=2).transpose(1, 2, 0, 3).reshape(P, -1),
        "mix_pre3": columns(i["norm_mix_pre_3"][0]), "q_norm": columns(i["q_norm_3"][0]),
        "kv_norm": columns(i["kv_norm_3"][0]),
        "conv3": i["conv_w_3"][0, :, 0].reshape(TAPS3, KD, P).transpose(2, 1, 0).reshape(P, -1),
        "conv_b": columns(i["conv_b_3"][0]), "ln3_g": columns(i["conv_ln_g_3"][0]),
        "ln3_b": columns(i["conv_ln_b_3"][0]), "b_pw2": columns(i["b_pw2_3"][0]),
        "mix_post3": columns(i["norm_mix_post_3"][0]), "mlp_pre3": columns(i["norm_mlp_pre_3"][0]),
        "mlp_post3": columns(i["norm_mlp_post_3"][0]),
    }
    for name, n in VECTORS:
        assert col[name].shape == (P, n), name
    return np.ascontiguousarray(np.concatenate([col[name] for name, _ in VECTORS], axis=1))


def constants():
    r = np.arange(P)
    row, colm = r[:, None], r[None, :]
    f = lambda a: np.broadcast_to(a, (P, a.shape[-1])).astype(np.float32)
    level, levelt = [], []
    for n in range(INV_LEVELS):
        b = 1 << n
        m = (row // (2 * b) == colm // (2 * b)) & (row % (2 * b) >= b) & (colm % (2 * b) < b)
        level.append(m)
        levelt.append(m.T)
    swap = row == np.where(colm % 64 < 32, colm + 32, colm - 32)
    j = r % 32
    c = {
        "ident": f(row == colm), "ones": f(np.ones((P, P))), "ones64": f(row // 64 == colm // 64),
        "le": f(row <= colm), "lt": f(row < colm),
        "blk_le": f((row // 32 == colm // 32) & (row <= colm)),
        "blk_ge": f((row // 32 == colm // 32) & (row >= colm)),
        "future": f(np.where(colm > row, -1e30, 0.0)), "swap": f(swap),
        "iota": f(np.arange(T)[None]), "reset": f((np.arange(T) % CHUNK1 != 0)[None]),
        "tok": f(row + P * np.arange(4)[None]), "own16": f(row == np.arange(16)[None]),
        "vblk": f(row // 32 == np.arange(4)[None]),
        "eps": f(np.array([[1e-6, 64e-5, 20 * np.log(2) / 2, 0.0]])),
        "invf": (10000.0 ** (-(2 * j.astype(np.float32)) / 64)).astype(np.float32)[:, None],
        "sgn": np.where(r % 64 < 32, -1.0, 1.0).astype(np.float32)[:, None],
        "onerow": f(np.ones((1, T))),
    }
    for name, n in CONSTANTS:
        assert c[name].shape == (P, n), name
    c = np.concatenate([c[name] for name, _ in CONSTANTS], axis=1)
    return np.ascontiguousarray(c), f(np.concatenate(level + levelt, axis=1))


def kernel(**inputs):
    import concourse.bacc as _bacc
    from concourse.bass_utils import run_bass_kernel_spmd as _run

    i = {n: np.asarray(a) for n, a in inputs.items()}
    const, levels = constants()
    arrays = {
        "x": i["x"][0].T.reshape(KD, P, T).transpose(1, 0, 2),
        "ctx": i["ctx"][0].T.reshape(KD, P, TC).transpose(1, 0, 2),
        "vec": vectors(i), "const": const, "levels": levels, "pos": i["positions_3"], "weights": weight_stream(i),
    }
    arrays = {f"in_{n}": np.ascontiguousarray(a) for n, a in arrays.items()}
    nc = _bacc.Bacc("TRN2", target_bir_lowering=False, num_devices=1)
    args = [nc.dram_tensor(n, a.shape, mybir.dt.from_np(a.dtype), kind="ExternalInput").ap() for n, a in arrays.items()]
    out = nc.dram_tensor("out_y", (P, KD, T), F32, kind="ExternalOutput").ap()
    three_blocks(nc, *args, out)
    got = _run(nc, [arrays], core_ids=[0]).results[0]["out_y"]
    return np.ascontiguousarray(got.transpose(1, 0, 2).reshape(1, D, T).transpose(0, 2, 1))
```
